# Optimizing a Trainium2 kernel written in Bass

```python
import jax, jax.numpy as jnp
from jax import lax
import numpy as np

D_MODEL = 1024
BATCH = 1
SEQ = 256
DEPTH = 1
DEC_BATCH = 1
DEC_SEQ = 512
PAST_LEN = 128

GRID_W = 64
D_MIX = D_MODEL
D_ATTN = D_MIX // 2
D_CONV = D_MIX - D_ATTN
HEAD_DIM = 64
N_HEADS = D_ATTN // HEAD_DIM
NA_ROWS_MAX = 8
NA_COLS = 16
CONV_WIDTH = 31
N_GROUPS = 4
EXPERTS_PER_GROUP = 8
N_EXPERTS = N_GROUPS * EXPERTS_PER_GROUP
TOP_K = 2
D_EXPERT = D_MODEL // 2
MOE_BLOCK = 128
EPS = 1e-6
D_IN = 3 * D_ATTN + 2 * D_CONV

kernel_name = 'hymba_natten_conformer_hmoe_encoder'

def rms_norm(x, g):
    xf = x.astype(jnp.float32)
    y = xf * lax.rsqrt(jnp.mean(xf * xf, axis=-1, keepdims=True) + EPS)
    return (y * g.astype(jnp.float32)).astype(x.dtype)

def layer_norm(x, g, b):
    xf = x.astype(jnp.float32)
    mu = jnp.mean(xf, axis=-1, keepdims=True)
    xc = xf - mu
    var = jnp.mean(xc * xc, axis=-1, keepdims=True)
    y = xc * lax.rsqrt(var + EPS) * g.astype(jnp.float32) + b.astype(jnp.float32)
    return y.astype(x.dtype)

def neighbourhood_attention(q, k, v, rpb):
    B, L, H, Dh = q.shape
    rows = L // GRID_W
    kr = min(NA_ROWS_MAX, rows)
    scale = HEAD_DIM ** -0.5
    qg = q.reshape(B, rows, GRID_W, H, Dh)
    kg = k.reshape(B, rows, GRID_W, H, Dh)
    vg = v.reshape(B, rows, GRID_W, H, Dh)
    col = jnp.arange(GRID_W)
    col_start = jnp.clip(col - NA_COLS // 2, 0, GRID_W - NA_COLS)
    col_idx = col_start[:, None] + jnp.arange(NA_COLS)[None, :]
    col_off = col_idx - col[:, None] + (NA_COLS - 1)
    rpb_cols = rpb[:, :, col_off]

    def row_block(args):
        q_r, r = args
        r_start = jnp.clip(r - kr // 2, 0, rows - kr)
        k_rows = lax.dynamic_slice_in_dim(kg, r_start, kr, axis=1)
        v_rows = lax.dynamic_slice_in_dim(vg, r_start, kr, axis=1)
        k_win = k_rows[:, :, col_idx]
        v_win = v_rows[:, :, col_idx]
        s = jnp.einsum('bqhd,brqjhd->bhqrj', q_r, k_win).astype(jnp.float32) * scale
        row_off = r_start + jnp.arange(kr) - r + (NA_ROWS_MAX - 1)
        bias = jnp.transpose(rpb_cols[:, row_off], (0, 2, 1, 3))
        s = s + bias[None].astype(jnp.float32)
        p = jax.nn.softmax(s.reshape(B, H, GRID_W, kr * NA_COLS), axis=-1)
        p = p.reshape(B, H, GRID_W, kr, NA_COLS).astype(v.dtype)
        return jnp.einsum('bhqrj,brqjhd->bqhd', p, v_win)

    out = lax.map(row_block, (jnp.moveaxis(qg, 1, 0), jnp.arange(rows)))
    return jnp.moveaxis(out, 0, 1).reshape(B, L, H * Dh)

def conformer_conv(u, w_dw, b_dw, ln_g, ln_b):
    a, gt = jnp.split(u, 2, axis=-1)
    z = a * jax.nn.sigmoid(gt)
    z = lax.conv_general_dilated(
        z, w_dw[:, None, :], window_strides=(1,),
        padding=[(CONV_WIDTH // 2, CONV_WIDTH // 2)],
        dimension_numbers=('NWC', 'WIO', 'NWC'),
        feature_group_count=D_CONV) + b_dw
    z = layer_norm(z, ln_g, ln_b)
    return jax.nn.silu(z)

def hier_moe(h, w_group, b_group, w_expert, b_expert, w_gate, w_up, w_down):
    T, D = h.shape
    hf = h.astype(jnp.float32)
    g_logits = hf @ w_group.astype(jnp.float32) + b_group.astype(jnp.float32)
    g_prob = jax.nn.softmax(g_logits, axis=-1)
    g_sel = jnp.argmax(g_logits, axis=-1)
    p_g = jnp.take_along_axis(g_prob, g_sel[:, None], axis=1)[:, 0]
    e_all = jnp.einsum('td,gde->tge', hf, w_expert.astype(jnp.float32)) + b_expert.astype(jnp.float32)
    e_logits = jnp.take_along_axis(e_all, g_sel[:, None, None], axis=1)[:, 0]
    top_v, top_j = lax.top_k(e_logits, TOP_K)
    gates = p_g[:, None] * jax.nn.softmax(top_v, axis=-1)
    expert_idx = (g_sel[:, None] * EXPERTS_PER_GROUP + top_j).astype(jnp.int32)

    A = T * TOP_K
    flat_e = expert_idx.reshape(A)
    flat_tok = jnp.arange(A, dtype=jnp.int32) // TOP_K
    order = jnp.argsort(flat_e)
    sorted_e = flat_e[order]
    counts = jnp.bincount(flat_e, length=N_EXPERTS).astype(jnp.int32)
    padded = ((counts + MOE_BLOCK - 1) // MOE_BLOCK) * MOE_BLOCK
    seg_start = jnp.cumsum(counts) - counts
    pad_end = jnp.cumsum(padded)
    pad_start = pad_end - padded
    rank = jnp.arange(A, dtype=jnp.int32) - seg_start[sorted_e]
    dest = pad_start[sorted_e] + rank
    n_blocks = A // MOE_BLOCK + N_EXPERTS
    P = n_blocks * MOE_BLOCK
    buf_tok = jnp.full((P,), T, dtype=jnp.int32).at[dest].set(flat_tok[order])
    h_pad = jnp.concatenate([h, jnp.zeros((1, D), h.dtype)], axis=0)
    xb = h_pad[buf_tok].reshape(n_blocks, MOE_BLOCK, D)
    block_start = jnp.arange(n_blocks, dtype=jnp.int32) * MOE_BLOCK
    block_e = jnp.clip(jnp.searchsorted(pad_end, block_start, side='right'), 0, N_EXPERTS - 1)

    def expert_block(args):
        x_b, e = args
        hid = jax.nn.silu(x_b @ w_gate[e]) * (x_b @ w_up[e])
        return hid @ w_down[e]

    yb = lax.map(expert_block, (xb, block_e)).reshape(P, D)
    dest_orig = jnp.zeros((A,), jnp.int32).at[order].set(dest)
    y_assign = yb[dest_orig].reshape(T, TOP_K, D)
    return jnp.einsum('tkd,tk->td', y_assign, gates.astype(h.dtype))

def encoder_trunk(x, norm1_g, w_in, rpb, attn_out_g, conv_w, conv_b, conv_ln_g, conv_ln_b,
                  conv_out_g, w_out, norm2_g, w_group, b_group, w_expert, b_expert,
                  w_e_gate, w_e_up, w_e_down, final_g):
    B, L, _ = x.shape
    for l in range(DEPTH):
        h = rms_norm(x, norm1_g[l])
        u = h @ w_in[l]
        q, k, v, uc = jnp.split(u, [D_ATTN, 2 * D_ATTN, 3 * D_ATTN], axis=-1)
        q = q.reshape(B, L, N_HEADS, HEAD_DIM)
        k = k.reshape(B, L, N_HEADS, HEAD_DIM)
        v = v.reshape(B, L, N_HEADS, HEAD_DIM)
        a = neighbourhood_attention(q, k, v, rpb[l])
        c = conformer_conv(uc, conv_w[l], conv_b[l], conv_ln_g[l], conv_ln_b[l])
        m = jnp.concatenate([rms_norm(a, attn_out_g[l]), rms_norm(c, conv_out_g[l])], axis=-1)
        x = x + m @ w_out[l]
        h = rms_norm(x, norm2_g[l]).reshape(B * L, D_MODEL)
        x = x + hier_moe(h, w_group[l], b_group[l], w_expert[l], b_expert[l],
                         w_e_gate[l], w_e_up[l], w_e_down[l]).reshape(B, L, D_MODEL)
    return rms_norm(x, final_g)

def setup_inputs(seed: int = 0) -> dict:
    key = jax.random.key(seed)
    ks = jax.random.split(key, 24)
    f32 = jnp.float32
    nrm = lambda k, s, sc: jax.random.normal(k, s, f32) * sc
    return {
        'x_prompt': nrm(ks[0], (BATCH, SEQ, D_MODEL), 1.0),
        'x_sample': nrm(ks[1], (DEC_BATCH, DEC_SEQ, D_MODEL), 1.0),
        'norm1_g': 1.0 + nrm(ks[2], (DEPTH, D_MODEL), 0.02),
        'w_in': nrm(ks[3], (DEPTH, D_MODEL, D_IN), D_MODEL ** -0.5),
        'rpb': nrm(ks[4], (DEPTH, N_HEADS, 2 * NA_ROWS_MAX - 1, 2 * NA_COLS - 1), 0.1),
        'attn_out_g': 1.0 + nrm(ks[5], (DEPTH, D_ATTN), 0.02),
        'conv_w': nrm(ks[6], (DEPTH, CONV_WIDTH, D_CONV), CONV_WIDTH ** -0.5),
        'conv_b': nrm(ks[7], (DEPTH, D_CONV), 0.02),
        'conv_ln_g': 1.0 + nrm(ks[8], (DEPTH, D_CONV), 0.02),
        'conv_ln_b': nrm(ks[9], (DEPTH, D_CONV), 0.02),
        'conv_out_g': 1.0 + nrm(ks[10], (DEPTH, D_CONV), 0.02),
        'w_out': nrm(ks[11], (DEPTH, D_MIX, D_MODEL), D_MIX ** -0.5),
        'norm2_g': 1.0 + nrm(ks[12], (DEPTH, D_MODEL), 0.02),
        'w_group': nrm(ks[13], (DEPTH, D_MODEL, N_GROUPS), D_MODEL ** -0.5),
        'b_group': nrm(ks[14], (DEPTH, N_GROUPS), 0.01),
        'w_expert': nrm(ks[15], (DEPTH, N_GROUPS, D_MODEL, EXPERTS_PER_GROUP), D_MODEL ** -0.5),
        'b_expert': nrm(ks[16], (DEPTH, N_GROUPS, EXPERTS_PER_GROUP), 0.01),
        'w_e_gate': nrm(ks[17], (DEPTH, N_EXPERTS, D_MODEL, D_EXPERT), D_MODEL ** -0.5),
        'w_e_up': nrm(ks[18], (DEPTH, N_EXPERTS, D_MODEL, D_EXPERT), D_MODEL ** -0.5),
        'w_e_down': nrm(ks[19], (DEPTH, N_EXPERTS, D_EXPERT, D_MODEL), D_EXPERT ** -0.5),
        'final_g': 1.0 + nrm(ks[20], (D_MODEL,), 0.02),
    }

def reference(x_prompt, x_sample, norm1_g, w_in, rpb, attn_out_g, conv_w, conv_b, conv_ln_g,
              conv_ln_b, conv_out_g, w_out, norm2_g, w_group, b_group, w_expert, b_expert,
              w_e_gate, w_e_up, w_e_down, final_g):
    y_prompt = encoder_trunk(x_prompt, norm1_g, w_in, rpb, attn_out_g, conv_w, conv_b, conv_ln_g,
                             conv_ln_b, conv_out_g, w_out, norm2_g, w_group, b_group, w_expert,
                             b_expert, w_e_gate, w_e_up, w_e_down, final_g)
    y_sample = encoder_trunk(x_sample, norm1_g, w_in, rpb, attn_out_g, conv_w, conv_b, conv_ln_g,
                             conv_ln_b, conv_out_g, w_out, norm2_g, w_group, b_group, w_expert,
                             b_expert, w_e_gate, w_e_up, w_e_down, final_g)
    return (y_prompt, y_sample)


_drawn_inputs = setup_inputs


def setup_inputs(seed=0):
    import zlib

    import numpy as np

    out = dict(_drawn_inputs(seed))
    spreads = {}
    factors = {'conv_ln_g': 2.76,
     'conv_out_g': 2.671,
     'b_group': 15.766,
     'b_expert': 15.764,
     'final_g': 8.711,
     'attn_out_g': 4.898,
     'conv_ln_b': 5.516,
     'norm2_g': 3.916}
    for name, (base, spread) in spreads.items():
        noise = np.random.default_rng([zlib.crc32(name.encode()), seed]).standard_normal(out[name].shape)
        drawn = base * np.exp(spread * noise) if base else spread * noise
        out[name] = __import__('jax').numpy.asarray(drawn.astype(out[name].dtype))
    for name, factor in factors.items():
        out[name] = (out[name] * factor).astype(out[name].dtype)
    return out
```

```python
from contextlib import ExitStack

import numpy as np

import concourse.bass as bass
from concourse import mybir

ALU = mybir.AluOpType
ACT = mybir.ActivationFunctionType
F32 = mybir.dt.float32
I32 = mybir.dt.int32
U32 = mybir.dt.uint32
AX = mybir.AxisListType

P = 128
D = 1024
KD = D // P
GRID = 64
LS, LP = 512, 256
T = LS + LP
NT = T // P
NTS = LS // P
RS, RP = LS // GRID, LP // GRID
H, DH = 8, 64
DA = H * DH
JC = (D - DA) // P
TAPS = 31
HALO = TAPS // 2
EPS = 1e-6
NEG = -1e30
G, EG = 4, 8
E = G * EG
F = 512
KF = F // P
BLK = 64
MAXB = 2 * T // BLK + E
XROWS = -(-(MAXB + 1) * BLK // P) * P
ZERO_TILES = -(-XROWS // P // 8)
NR = G + E
MAXN = T // BLK
SLOTS = 3

RPBW = 127
RPBROWS = 15
VARIANTS = [(RS, 16, 0, 0, 32), (RS, 16, 16, 8, 32), (RS, 16, 48, 32, 32), (RP, 32, 0, 0, 64), (RP, 32, 32, 0, 64)]
NV = len(VARIANTS)
VARIANT_OF = [0, 1, 1, 2, 3, 4]
KEYS_AT = [0, 64, 192, 256, LS, LS]
VALUES_AT = [(0, 2), (1, 3), (3, 5), (4, 6), (7, 8), (7, 8)]
STRIP_ROWS = [2 * v[0] - 1 for v in VARIANTS]
STRIP_SIZE = [v[1] * n * v[4] for v, n in zip(VARIANTS, STRIP_ROWS)]
STRIP_AT = [sum(STRIP_SIZE[:i]) for i in range(NV)]
STRIPS = sum(STRIP_SIZE)

V_N1, V_CW, V_CB, V_LG, V_LB, V_GO = 0, KD, KD + JC * TAPS, KD + JC * TAPS + JC, KD + JC * TAPS + 2 * JC, KD + JC * TAPS + 3 * JC
NVEC = V_GO + KD

CHUNKS = [("conv", 0), ("v", 0), ("v", 1), ("qk", 0), ("conv", 1), ("qk", 1), ("conv", 2), ("qk", 2), ("qk", 3), ("conv", 3)]
WBUFS = 3
OUT_CHUNKS = 4


def chunk_columns(kind, i):
    if kind == "conv":
        return 3 * DA + P * i, 3 * DA + (D - DA) + P * i
    if kind == "qk":
        return P * i, DA + P * i
    return 2 * DA + 2 * P * i, 2 * DA + 2 * P * i + P


def plan():
    order, att, taps, left, qk_done = [], 0, [], NATT, 0
    for c, (kind, i) in enumerate(CHUNKS):
        for g in range(NT if kind == "v" else 4):
            for half in range(2):
                order.append(("win", c, g, half))
                if att < min(NATT, 12 * qk_done):
                    order.append(("att", att))
                    att += 1
                for _ in range(3 if kind == "v" or g < 2 else 2):
                    if taps:
                        order.append(("tap", *taps.pop(0)))
        if kind == "qk":
            qk_done += 1
        if kind == "conv":
            taps += [(i, k) for k in range(TAPS)]
    while att < NATT or taps:
        if att < NATT:
            order.append(("att", att))
            att += 1
        for _ in range(2):
            if taps:
                order.append(("tap", *taps.pop(0)))
    return order


NATT = H * NT + 2
ORDER = plan()


def accumulation_groups():
    at, n = {}, 0
    for c, (kind, _) in enumerate(CHUNKS):
        for g in range(NT if kind == "v" else 4):
            at[c, g] = n
            n += 1
    return at


GROUP_AT = accumulation_groups()
RAW_AFTER = {3: (0, 1), 5: (2, 3), 7: (4,), 8: (5,), 9: (6,), 10: (7,)}


def taken_out():
    out, copies = {}, 0
    for (c, g), n in GROUP_AT.items():
        kind, i = CHUNKS[c]
        if kind == "conv":
            out[n] = ("sig" if g % 2 else "z", 2 * i + g // 2 + 1)
        else:
            copies += 1
            out[n] = ("copy", copies)
    return out


TAKEN_OUT = taken_out()


def copies_after(kind, i):
    c = CHUNKS.index((kind, i))
    return TAKEN_OUT[GROUP_AT[c, (NT if kind == "v" else 4) - 1]][1]


def arrivals():
    at, count = [], [0] * WBUFS
    for c in range(len(CHUNKS) + OUT_CHUNKS):
        count[c % WBUFS] += 32 if c < len(CHUNKS) else 16
        at.append(count[c % WBUFS])
    return at


WIN_TARGET = arrivals()


def encoder(nc, x_prompt, x_sample, w_in, rpb, vectors, w_out, norm2, router_w, router_b,
            w_gate, w_up, w_down, final_g, y_prompt, y_sample):
    strips = nc.dram_tensor("strips", (H, STRIPS), F32, kind="Internal").ap()
    rows = nc.dram_tensor("rows", (XROWS, D), F32, kind="Internal").ap()

    def rows_of(x_p, x_s, t):
        if t < NTS:
            n = P // RS
            return x_s[0].rearrange("(r c) d -> c r d", c=GRID)[n * t:n * t + n]
        n = P // RP
        return x_p[0].rearrange("(r c) d -> c r d", c=GRID)[n * (t - NTS):n * (t - NTS) + n]

    with ExitStack() as ctx:
        def sb(name, shape, dt=F32):
            return ctx.enter_context(nc.sbuf_tensor(name, shape, dt))

        def sem(name):
            return ctx.enter_context(nc.semaphore(name))

        ring = sb("ring", [P, 2, (2 * KD * F + KF * D)])
        slot0, slot1 = ring[:, 0, :], ring[:, 1, :]
        hT = slot1[:, 0:KD * T].rearrange("p (k n) -> p k n", k=KD)
        mT = hT
        wst = slot1[:, KD * T:].rearrange("p (b k n) -> p b k n", b=WBUFS, k=KD)
        qT = slot0[:, 0:4 * T].rearrange("p (j n) -> p j n", j=4)
        kT = slot0[:, 4 * T:8 * T].rearrange("p (j n) -> p j n", j=4)
        vals = slot0[:, 8 * T:8 * T + 9 * DA].rearrange("p (j n) -> p j n", j=9)
        mask = slot0[:, 8 * T + 9 * DA:8 * T + 9 * DA + NV * 256].rearrange("p (v n) -> p v n", v=NV)
        gath = slot0[:, 0:4 * D].rearrange("p (b j d) -> p b j d", b=2, j=2)

        x = sb("x", [P, NT, D])
        ZW = HALO + LS + HALO + LP + HALO
        CW = ZW - 2 * HALO
        MID = 2 * ZW + 2 * CW + JC * T + 4 * NV * 256
        big = sb("big", [P, MID + NT * DA + 3 * D])
        mid, attn, scr = big[:, 0:MID], big[:, MID:MID + NT * DA], big[:, MID + NT * DA:]
        attn = attn.rearrange("p (t n) -> p t n", t=NT)
        zpad = mid[:, 0:2 * ZW].rearrange("p (b n) -> p b n", b=2)
        conv = mid[:, 2 * ZW:2 * ZW + 2 * CW].rearrange("p (b n) -> p b n", b=2)
        o = 2 * ZW + 2 * CW
        conv_out = mid[:, o:o + JC * T].rearrange("p (j n) -> p j n", j=JC)
        zn = mid[:, o:o + NT * 512].rearrange("p (t n) -> p t n", t=NT)
        o += JC * T
        raw = mid[:, o:o + 2 * NV * 256].rearrange("p (b v n) -> p b v n", b=2, v=NV)
        bias = mid[:, o + 2 * NV * 256:].rearrange("p (b v n) -> p b v n", b=2, v=NV)
        h2 = mid[:, 0:NT * D].rearrange("p (t d) -> p t d", t=NT)
        h2T = mid[:, NT * D:NT * D + 2 * D].rearrange("p (b k n) -> p b k n", b=2, k=KD)
        slot2_gu, slot2_dn = big[:, (NT + 2) * D:(NT + 2) * D + 2 * KD * F], big[:, 0:KF * D]
        gus = [slot0[:, 0:2 * KD * F], slot1[:, 0:2 * KD * F], slot2_gu]
        dns = [slot0[:, 2 * KD * F:], slot1[:, 2 * KD * F:], slot2_dn]
        gate_w = [g[:, 0:KD * F].rearrange("p (k f) -> p k f", k=KD) for g in gus]
        up_w = [g[:, KD * F:].rearrange("p (k f) -> p k f", k=KD) for g in gus]
        down_w = [d.rearrange("p (k d) -> p k d", k=KF) for d in dns]
        o = KF * D
        xb = big[0:BLK, o:o + D]
        xT = big[:, o + D:o + D + KD * BLK].rearrange("p (k n) -> p k n", k=KD)
        sG = big[64:128, o + 2 * D:o + 2 * D + F]
        hb = big[0:BLK, o + 2 * D + F:o + 2 * D + 2 * F]
        hbT = big[:, o + 3 * D:o + 3 * D + KF * BLK].rearrange("p (k n) -> p k n", k=KF)
        yb = big[:, o + 3 * D + 512:o + 4 * D]
        xs = scr[:, 0:2 * D].rearrange("p (b d) -> p b d", b=2)
        junk = scr[:, 2 * D:3 * D]
        neg_s = scr[:, 0:512].rearrange("p (b n) -> p b n", b=2)
        prob = scr[:, 512:1024].rearrange("p (b n) -> p b n", b=2)
        probT = scr[:, 1024:1536].rearrange("p (b n) -> p b n", b=2)
        sig = scr[:, 1536:2048]
        sq = scr[:, 0:1024].rearrange("p (b n) -> p b n", b=2)
        n2 = sb("n2", [P, D])
        fin_g = n2[:]
        zeros = sb("zeros", [P, D])
        vec = sb("vec", [P, NVEC])
        wr = sb("wr", [P, KD, NR])
        br = sb("br", [P, NR])
        ident = sb("ident", [P, P])
        tri = sb("tri", [P, P])
        ones = sb("ones", [P, P])
        w8 = sb("w8", [P, EG])
        w4 = sb("w4", [P, G])
        thr = sb("thr", [P, MAXN - 1])
        half_neg = sb("half_neg", [P, NT])
        ss1 = sb("ss1", [P, NT]); r1 = sb("r1", [P, NT])
        ssa = sb("ssa", [P, NT]); ra = sb("ra", [P, NT])
        ssc = sb("ssc", [P, NT]); rc = sb("rc", [P, NT])
        ss2 = sb("ss2", [P, NT]); r2 = sb("r2", [P, NT])
        ssf = sb("ssf", [P, NT]); rf = sb("rf", [P, NT])
        bst = sb("bst", [P, NT, 6]); mv = sb("mv", [P, NT, 2]); rl = sb("rl", [P, NT])
        nmax = sb("nmax", [P, 2]); rsum = sb("rsum", [P, 2, NT]); rinv = sb("rinv", [P, 2, NT])
        lg = sb("lg", [P, NT, NR])
        g1 = sb("g1", [P, NT]); gd = sb("gd", [P, NT, G]); ge = sb("ge", [P, NT, G])
        gpi = sb("gpi", [P, NT]); gp = sb("gp", [P, NT])
        t4 = sb("t4", [P, NT, G]); t1 = sb("t1", [P, NT]); ohg = sb("ohg", [P, NT, G])
        es = sb("es", [P, NT, EG]); es2 = sb("es2", [P, NT, EG])
        m1 = sb("m1", [P, NT]); m2 = sb("m2", [P, NT]); t8 = sb("t8", [P, NT, EG])
        oh = sb("oh", [P, 2, NT, EG])
        dd = sb("dd", [P, NT]); ex = sb("ex", [P, NT]); gate1 = sb("gate1", [P, NT]); gate2 = sb("gate2", [P, NT])
        o = NT * D
        el = mid[:, o:o + NT * E].rearrange("p (t g e) -> p t g e", t=NT, g=G)
        sel = mid[:, o + NT * E:o + 3 * NT * E].rearrange("p (j t e) -> p j t e", j=2, t=NT)
        both = mid[:, o + 3 * NT * E:o + 4 * NT * E].rearrange("p (t e) -> p t e", t=NT)
        pos = mid[:, o + 4 * NT * E:o + 5 * NT * E].rearrange("p (t e) -> p t e", t=NT)
        posd = mid[:, o + 5 * NT * E:o + 6 * NT * E].rearrange("p (t e) -> p t e", t=NT)
        cmpb = mid[:, o + 6 * NT * E:o + 6 * NT * E + E * (MAXN - 1)].rearrange("p (e n) -> p e n", e=E)
        cnt = sb("cnt", [P, E]); nblk = sb("nblk", [P, E])
        onesr = sb("onesr", [P, E]); endb = sb("endb", [P, E]); st64 = sb("st64", [P, E])
        destf = sb("destf", [P, 2, NT])
        dest = sb("dest", [P, 2, NT], U32)
        table = sb("table", [1, 3 * E], I32)

        ps = ctx.enter_context(nc.psum_tensor("ps", [P, 8, 512], F32))

        x_in = [sem(f"x_in{t}") for t in range(NT)]
        vec_in, small_in, n2_in, fin_in = sem("vec_in"), sem("small_in"), sem("n2_in"), sem("fin_in")
        win_in = [sem(f"win_in{b}") for b in range(WBUFS)]
        strip_out, raw_in = sem("strip_out"), [sem("raw_in0"), sem("raw_in1")]
        zero_out = sem("zero_out")
        consts = sem("consts")
        sq1, root1, xs_ready, xps, h_ready = sem("sq1"), sem("root1"), sem("xs_ready"), sem("xps"), sem("h_ready")
        win_done = sem("win_done")
        copy_done = sem("copy_done")
        sig_ready, z_done, conv_done = sem("sig_ready"), sem("z_done"), sem("conv_done")
        bias_ready, zeros_ready, ssc_ready = sem("bias_ready"), sem("zeros_ready"), sem("ssc_ready")
        s_done, neg_done, exp_done, pt_done, ptc_done, o_done, attn_done = (
            sem("s_done"), sem("neg_done"), sem("exp_done"), sem("pt_done"), sem("ptc_done"), sem("o_done"), sem("attn_done"))
        dch = sem("dch")
        pch = sem("pch")
        ct_done, stat_done, rootl, zn_ready, zt_done, silu_done, sq_ready, ssc_done, ssa_done, rootc, roota = (
            sem("ct_done"), sem("stat_done"), sem("rootl"), sem("zn_ready"), sem("zt_done"), sem("silu_done"),
            sem("sq_ready"), sem("ssc_done"), sem("ssa_done"), sem("rootc"), sem("roota"))
        at_done, mta_done = sem("at_done"), sem("mta_done")
        wout_scaled, wout_done, x2_done = sem("wout_scaled"), sem("wout_done"), sem("x2_done")
        sq2, root2, h2_ready, h2t_done, h2t_ready, lg_done = (
            sem("sq2"), sem("root2"), sem("h2_ready"), sem("h2t_done"), sem("h2t_ready"), sem("lg_done"))
        gd_ready, ge_ready, both_ready, rank_done, dd_ready, ex_ready, dest_ready, table_ready = (
            sem("gd_ready"), sem("ge_ready"), sem("both_ready"), sem("rank_done"), sem("dd_ready"), sem("ex_ready"),
            sem("dest_ready"), sem("table_ready"))
        scattered = sem("scattered")
        gate_in = [[sem(f"gate_in{s}{q}") for q in range(2)] for s in range(SLOTS)]
        up_in = [[sem(f"up_in{s}{q}") for q in range(2)] for s in range(SLOTS)]
        dn_in = [[sem(f"dn_in{s}{q}") for q in range(2)] for s in range(SLOTS)]
        xb_in, xt_ps, xt_ready, gu_done, sg_ready, hb_ready, ht_ps, ht_ready, y_done, y_evac, y_out = (
            sem("xb_in"), sem("xt_ps"), sem("xt_ready"), sem("gu_done"), sem("sg_ready"), sem("hb_ready"),
            sem("ht_ps"), sem("ht_ready"), sem("y_done"), sem("y_evac"), sem("y_out"))
        pe_passed, pool_passed = sem("pe_passed"), sem("pool_passed")
        gath_in = [sem("gath_in0"), sem("gath_in1")]
        xf_done, sqf, rootf, fin_done, out_done = sem("xf_done"), sem("sqf"), sem("rootf"), sem("fin_done"), sem("out_done")

        block = ctx.enter_context(nc.Block())

        def columns(g):
            return g % 2, (slice(0, LS) if g < 2 else slice(LS, T)), (LS if g < 2 else LP)

        def scale_w_out(pool, n):
            c = len(CHUNKS) + n
            pool.wait_ge(win_in[c % WBUFS], WIN_TARGET[c])
            w = wst[:, c % WBUFS, :, :]
            nc.gpsimd.tensor_tensor(w, w, vec[:, V_GO:V_GO + KD].unsqueeze(2).to_broadcast([P, KD, 2 * P]),
                                    ALU.mult).then_inc(wout_scaled, 1)

        def logits(pe, t):
            pe.wait_ge(h2t_ready, t + 1)
            for k in range(KD):
                mm = pe.matmul(ps[:, 6, t * NR:(t + 1) * NR], h2T[:, t % 2, k, :], wr[:, k, :],
                               start=(k == 0), stop=(k == KD - 1))
            mm.then_inc(lg_done, 1)

        @block.sync
        def _(sp):
            def load_win(c):
                b = c % WBUFS
                if c >= WBUFS:
                    last = c - WBUFS
                    sp.wait_ge(win_done, GROUP_AT[last, (NT if CHUNKS[last][0] == "v" else 4) - 1] + 1)
                for sub, col in enumerate(chunk_columns(*CHUNKS[c])):
                    sp.dma_start(wst[:, b, :, sub * P:(sub + 1) * P],
                                 w_in[0, :, col:col + P].rearrange("(k p) n -> p k n", p=P)).then_inc(win_in[b], 16)

            def load_raw(h):
                for v, (R, nq, q0, k0, nk) in enumerate(VARIANTS):
                    src = bass.AP(strips.tensor, h * STRIPS + STRIP_AT[v] + (R - 1) * nk,
                                  [[STRIP_ROWS[v] * nk, nq], [-nk, R], [1, R * nk]])
                    sp.dma_start(raw[:, h % 2, v, :], src).then_inc(raw_in[h % 2], 16)

            for t in range(NT):
                sp.dma_start(x[:, t, :], rows_of(x_prompt, x_sample, t)).then_inc(x_in[t], 16)
                if t == 0:
                    sp.dma_start(vec[:], vectors).then_inc(vec_in, 16)
                if t == 2:
                    load_win(0)
            sp.dma_start(wr[:], router_w.rearrange("p (k n) -> p k n", k=KD)).then_inc(small_in, 16)
            sp.dma_start(br[:], bass.AP(router_b.tensor, 0, [[0, P], [1, NR]])).then_inc(small_in, 16)
            sp.dma_start(n2[:], bass.AP(norm2.tensor, 0, [[0, P], [1, D]])).then_inc(n2_in, 16)
            load_win(1)
            load_win(2)

            def heads_after(c):
                for h in RAW_AFTER.get(c, ()):
                    if h == 0:
                        sp.wait_ge(strip_out, 16 * H * NV)
                    if h >= 2:
                        sp.wait_ge(bias_ready, h - 1)
                    load_raw(h)

            for c in range(WBUFS, len(CHUNKS)):
                load_win(c)
                heads_after(c)
            for n in range(OUT_CHUNKS):
                c = len(CHUNKS) + n
                if n < WBUFS:
                    last = c - WBUFS
                    sp.wait_ge(win_done, GROUP_AT[last, 3] + 1)
                else:
                    sp.wait_ge(wout_done, NT * (n - WBUFS + 1))
                sp.dma_start(wst[:, c % WBUFS, :, :], w_out[0, :, 2 * P * n:2 * P * (n + 1)].rearrange(
                    "(k p) n -> p k n", p=P)).then_inc(win_in[c % WBUFS], 16)
                heads_after(c)

            def in_order(s):
                for q in range(2):
                    ks = slice(q * KD // 2, (q + 1) * KD // 2)
                    yield gate_in[s][q], gate_w[s], w_gate, ks
                    yield up_in[s][q], up_w[s], w_up, ks
                for q in range(2):
                    yield dn_in[s][q], down_w[s], w_down, slice(q * KF // 2, (q + 1) * KF // 2)

            def load(e, landed, to, w, ks):
                sp.dma_start(to[:, ks, :], w[0, bass.ds(e, 1)].rearrange(
                    "e (p k) f -> p (e k) f", p=P)[:, ks, :]).then_inc(landed, 16)

            def load_gate_up(e, s):
                for l in list(in_order(s))[0:4]:
                    load(e, *l)

            def load_down(e, s):
                for l in list(in_order(s))[4:]:
                    load(e, *l)

            def load_expert(i, s):
                e = SLOTS * i + s
                end = sp.value_load(table[0:1, bass.ds(e + (2 * E - SLOTS), 1)], min_val=1, max_val=MAXB)
                before = list(in_order((s - 1) % SLOTS))[-2:]
                loads = list(in_order(s))
                for n, l in enumerate(loads):
                    if n < 2:
                        sp.wait_ge(before[n][0], 16 * i + (16 if s else 0))
                    else:
                        sp.wait_ge(loads[n - 2][0], 16 * i + 16)
                    if n == 0:
                        sp.wait_ge(gu_done, end)
                    elif n == 4:
                        sp.wait_ge(y_done, end)
                    load(e, *l)

            sp.wait_ge(o_done, H * NT)
            load_gate_up(0, 0)
            load_down(0, 0)
            sp.wait_ge(wout_done, 1)
            load_gate_up(2, 2)
            sp.wait_ge(wout_done, NT * OUT_CHUNKS)
            load_gate_up(1, 1)
            load_down(1, 1)
            sp.wait_ge(scattered, 16 * 2 * NT)
            load_down(2, 2)
            sp.wait_ge(h2_ready, NT)
            sp.dma_start(fin_g, bass.AP(final_g.tensor, 0, [[0, P], [1, D]])).then_inc(fin_in, 16)
            sp.wait_ge(table_ready, 1)
            with sp.Fori(1, E // SLOTS) as i:
                for s in range(SLOTS):
                    load_expert(i, s)
            for e in range(E // SLOTS * SLOTS, E):
                load_expert(e // SLOTS, e % SLOTS)
            for t in range(NT):
                sp.wait_ge(fin_done, t + 1)
                sp.dma_start(rows_of(y_prompt, y_sample, t), x[:, t, :]).then_inc(out_done, 16)
            sp.wait_ge(out_done, 16 * NT)

        @block.gpsimd
        def _(pool):
            n_link = [0]

            def link(ins):
                n_link[0] += 1
                ins.then_inc(pch, 1)
                pool.wait_ge(pch, n_link[0])

            link(nc.gpsimd.memset(ident[:], 0.0))
            link(nc.gpsimd.memset(tri[:], 0.0))
            nc.gpsimd.memset(half_neg[:], -0.5).then_inc(consts, 1)
            nc.gpsimd.affine_select(out=ident[:], in_=ident[:], compare_op=ALU.not_equal, fill=1.0, base=0,
                                    pattern=[[-1, P]], channel_multiplier=1).then_inc(consts, 1)
            nc.gpsimd.affine_select(out=tri[:], in_=tri[:], compare_op=ALU.is_ge, fill=1.0, base=0,
                                    pattern=[[-1, P]], channel_multiplier=1).then_inc(consts, 1)
            nc.gpsimd.memset(ones[:], 1.0).then_inc(consts, 1)
            nc.gpsimd.iota(w8[:], [[-1, EG]], base=EG, channel_multiplier=0,
                           allow_small_or_imprecise_dtypes=True).then_inc(consts, 1)
            nc.gpsimd.iota(w4[:], [[-1, G]], base=G, channel_multiplier=0,
                           allow_small_or_imprecise_dtypes=True).then_inc(consts, 1)
            nc.gpsimd.iota(thr[:], [[BLK, MAXN - 1]], base=BLK, channel_multiplier=0,
                           allow_small_or_imprecise_dtypes=True).then_inc(consts, 1)
            nc.gpsimd.memset(onesr[:], 1.0).then_inc(consts, 1)

            def root(out, in_, scale, ready, n):
                link(nc.gpsimd.tensor_scalar(out, in_, scale, EPS, ALU.mult, ALU.add))
                nc.gpsimd.tensor_tensor(out, out, half_neg[:, 0:n], ALU.pow).then_inc(ready, 1)

            pool.wait_ge(consts, 1)
            for t in range(NT):
                pool.wait_ge(sq1, t + 1)
                root(r1[:, t:t + 1], ss1[:, t:t + 1], 1.0 / D, root1, 1)

            link(nc.gpsimd.memset(mask[:], 0.0))
            for v, (R, nq, q0, k0, nk) in enumerate(VARIANTS):
                lo = mask[:, v, 0:(48 - k0) * R] if k0 + nk > 48 else mask[:, v, :]
                n = min(nk, 48 - k0)
                lo = lo.rearrange("p (c r) -> p c r", r=R)
                link(nc.gpsimd.affine_select(out=lo, in_=lo, compare_op=ALU.is_ge, fill=NEG,
                                             base=R * (k0 - q0 + 8) + R - 1, pattern=[[R, n], [0, R]],
                                             channel_multiplier=-1))
                s = max(0, 16 - k0)
                hi = mask[:, v, s * R:].rearrange("p (c r) -> p c r", r=R)
                link(nc.gpsimd.affine_select(out=hi, in_=hi, compare_op=ALU.is_ge, fill=NEG,
                                             base=R * (q0 - k0 + 7 - s), pattern=[[-R, nk - s], [0, R]],
                                             channel_multiplier=1))
            for h in range(H):
                b = h % 2
                pool.wait_ge(raw_in[b], 16 * NV * (h // 2 + 1))
                if h >= 2:
                    pool.wait_ge(neg_done, NT * (h - 1))
                for v0, v1, R in ((0, 3, RS), (3, 5, RP)):
                    dst = bias[:, b, v0:v1, :].rearrange("p v (c r) -> p v c r", r=R)
                    ins = nc.gpsimd.tensor_tensor(
                        dst, raw[:, b, v0:v1, :].rearrange("p v (r c) -> p v c r", r=R),
                        mask[:, v0:v1, :].rearrange("p v (c r) -> p v c r", r=R), ALU.add)
                ins.then_inc(bias_ready, 1)
                if h == 0:
                    pool.wait_ge(zeros_ready, 1)
                n = min(XROWS // P - ZERO_TILES * h, ZERO_TILES)
                pool.dma_start(rows[P * ZERO_TILES * h:P * (ZERO_TILES * h + n), :].rearrange("(n p) d -> p n d", p=P),
                               zeros[:].unsqueeze(1).to_broadcast([P, n, D])).then_inc(zero_out, 16)

            pool.wait_ge(stat_done, NT)
            root(rl[:], mv[:, :, 1], 1.0, rootl, NT)
            pool.wait_ge(ssa_done, NT)
            root(ra[:], ssa[:], 1.0 / DA, roota, NT)
            for n in range(2):
                scale_w_out(pool, n)
            for t in range(NT):
                pool.wait_ge(silu_done, JC * (t + 1))
                if t >= 2:
                    pool.wait_ge(ssc_done, t - 1)
                m = mT[:, JC:, t * P:(t + 1) * P]
                nc.gpsimd.tensor_tensor(sq[:, t % 2, :].rearrange("p (j n) -> p j n", j=JC), m, m,
                                        ALU.mult).then_inc(sq_ready, 1)
            scale_w_out(pool, 2)
            pool.wait_ge(ssc_ready, 1)
            root(rc[:], ssc[:], 1.0 / DA, rootc, NT)
            scale_w_out(pool, 3)
            for t in range(NT):
                pool.wait_ge(sq2, t + 1)
                root(r2[:, t:t + 1], ss2[:, t:t + 1], 1.0 / D, root2, 1)

            pool.wait_ge(zero_out, 16 * H)
            pool.wait_ge(dest_ready, 1)
            for t in range(NT):
                for j in range(2):
                    pool.indirect_dma_start(
                        out=rows, out_offset=bass.IndirectOffsetOnAxis(ap=dest[:, j, t:t + 1], axis=0),
                        in_=h2[:, t, :], in_offset=None).then_inc(scattered, 16)
            pool.wait_ge(scattered, 16 * 2 * NT)
            pool.wait_ge(table_ready, 1)
            total = pool.value_load(table[0:1, 3 * E - 1:3 * E], min_val=E, max_val=MAXB)

            def load_rows(b):
                pool.dma_start(xb, rows[bass.ds(b * BLK, BLK), :]).then_inc(xb_in, 16)

            load_rows(0)
            with pool.Fori(0, total) as b:
                pool.wait_ge(xt_ps, b + 1)
                load_rows(b + 1)
                pool.wait_ge(y_evac, 2 * b + 3)
                pool.dma_start(rows[bass.ds(b * BLK, BLK), :].rearrange("p (h c) -> h p c", h=2), yb).then_inc(y_out, 16)
            pool.wait_ge(y_out, 16 * total)
            pool.wait_ge(xb_in, 16 * total + 16)
            pool.sem_inc(pool_passed, 1)
            for t in range(NT):
                if t >= 2:
                    pool.wait_ge(xf_done, t - 1)
                for j in range(2):
                    pool.indirect_dma_start(
                        out=gath[:, t % 2, j, :], out_offset=None, in_=rows,
                        in_offset=bass.IndirectOffsetOnAxis(ap=dest[:, j, t:t + 1], axis=0)).then_inc(gath_in[t % 2], 16)
                if t >= 1:
                    pool.wait_ge(sqf, t)
                    root(rf[:, t - 1:t], ssf[:, t - 1:t], 1.0 / D, rootf, 1)
            pool.wait_ge(sqf, NT)
            root(rf[:, NT - 1:NT], ssf[:, NT - 1:NT], 1.0 / D, rootf, 1)

        @block.tensor
        def _(pe):
            pe.wait_ge(consts, 8)
            for t in range(NT):
                pe.wait_ge(xs_ready, t + 1)
                if t >= 2:
                    pe.wait_ge(h_ready, t - 1)
                for k in range(KD):
                    mm = pe.transpose(ps[:, 2 + 2 * (t % 2) + k // 4, (k % 4) * P:(k % 4 + 1) * P],
                                      xs[:, t % 2, k * P:(k + 1) * P], ident[:])
                mm.then_inc(xps, 1)
            pe.wait_ge(h_ready, NT)

            def win(c, g, half):
                kind, i = CHUNKS[c]
                n = GROUP_AT[c, g]
                if half == 0:
                    pe.wait_ge(win_in[c % WBUFS], WIN_TARGET[c])
                    if n >= 2:
                        who, count = TAKEN_OUT[n - 2]
                        pe.wait_ge({"z": z_done, "sig": sig_ready, "copy": copy_done}[who], count)
                for k in range(4 * half, 4 * half + 4):
                    if kind == "v":
                        mm = pe.matmul(ps[:, n % 2, 0:2 * P], hT[:, k, g * P:(g + 1) * P], wst[:, c % WBUFS, k, :],
                                       start=(k == 0), stop=(k == KD - 1))
                    else:
                        sub, cols, size = columns(g)
                        mm = pe.matmul(ps[:, n % 2, 0:size], wst[:, c % WBUFS, k, sub * P:(sub + 1) * P],
                                       hT[:, k, cols], start=(k == 0), stop=(k == KD - 1))
                if half:
                    mm.then_inc(win_done, 1)

            def scores(u):
                h, t = divmod(u, NT)
                p0 = (h % 2) * DH
                if t == 0:
                    pe.wait_ge(copy_done, copies_after("qk", h // 2))
                if u >= 2:
                    pe.wait_ge(neg_done, u - 1)
                pe.matmul(ps[:, 2 + u % 2, 0:256], qT[p0:p0 + DH, h // 2, t * P:(t + 1) * P],
                          kT[p0:p0 + DH, h // 2, KEYS_AT[t]:KEYS_AT[t] + 256], start=True, stop=True).then_inc(s_done, 1)

            def turn(u):
                pe.wait_ge(exp_done, u + 1)
                if u >= 2:
                    pe.wait_ge(ptc_done, u - 1)
                for c in range(2):
                    mm = pe.transpose(ps[:, 4 + u % 2, c * P:(c + 1) * P], prob[:, u % 2, c * P:(c + 1) * P], ident[:])
                mm.then_inc(pt_done, 1)

            def values(u):
                h, t = divmod(u, NT)
                pe.wait_ge(ptc_done, u + 1)
                if u == 0:
                    pe.wait_ge(copy_done, copies_after("v", 1))
                if t == 0 and h >= 2:
                    pe.wait_ge(attn_done, h - 1)
                for c in range(2):
                    mm = pe.matmul(ps[:, 6 + h % 2, t * DH:(t + 1) * DH], probT[:, u % 2, c * P:(c + 1) * P],
                                   vals[:, VALUES_AT[t][c], h * DH:(h + 1) * DH], start=(c == 0), stop=(c == 1))
                mm.then_inc(o_done, 1)

            for what, *a in ORDER:
                if what == "win":
                    win(*a)
                elif what == "att":
                    k, = a
                    if k < H * NT:
                        scores(k)
                    if 1 <= k <= H * NT:
                        turn(k - 1)
                    if k >= 2:
                        values(k - 2)

            pe.wait_ge(conv_done, JC)
            pe.wait_ge(copy_done, copies_after("qk", 3))
            pe.wait_ge(ptc_done, H * NT)
            for t in range(NT):
                for j in range(JC):
                    mm = pe.transpose(ps[:, t, j * P:(j + 1) * P], conv_out[:, j, t * P:(t + 1) * P], ident[:])
                mm.then_inc(ct_done, 1)
            pe.wait_ge(attn_done, H)
            for t in range(NT):
                if t >= 2:
                    pe.wait_ge(mta_done, t - 1)
                for j in range(JC):
                    mm = pe.transpose(ps[:, 6 + t % 2, j * P:(j + 1) * P], attn[:, t, j * P:(j + 1) * P], ident[:])
                mm.then_inc(at_done, 1)
            pe.wait_ge(mta_done, NT)
            for t in range(NT):
                pe.wait_ge(zn_ready, t + 1)
                if t >= 2:
                    pe.wait_ge(silu_done, JC * (t - 1))
                for j in range(JC):
                    mm = pe.transpose(ps[:, 6 + t % 2, j * P:(j + 1) * P], zn[:, t, j * P:(j + 1) * P], ident[:])
                mm.then_inc(zt_done, 1)
            pe.wait_ge(zn_ready, NT)
            for t in range(NT):
                pe.wait_ge(sq_ready, t + 1)
                for j in range(JC):
                    mm = pe.matmul(ps[:, 0, t:t + 1], sq[:, t % 2, j * P:(j + 1) * P], ones[:, 0:1],
                                   start=(j == 0), stop=(j == JC - 1))
                mm.then_inc(ssc_done, 1)
            for n in range(OUT_CHUNKS):
                c = len(CHUNKS) + n
                pe.wait_ge(wout_scaled, n + 1)
                for t in range(NT):
                    g = n * NT + t
                    if g >= 2:
                        pe.wait_ge(x2_done, g - 1)
                    for k in range(KD):
                        part = k // JC
                        mm = pe.matmul(ps[:, 2 + g % 2, part * 2 * P:(part + 1) * 2 * P], mT[:, k, t * P:(t + 1) * P],
                                       wst[:, c % WBUFS, k, :], start=(k % JC == 0), stop=(k % JC == JC - 1))
                    mm.then_inc(wout_done, 1)
            pe.wait_ge(x2_done, OUT_CHUNKS * NT)
            for t in range(NT):
                pe.wait_ge(h2_ready, t + 1)
                if t >= 2:
                    pe.wait_ge(h2t_ready, t - 1)
                for k in range(KD):
                    mm = pe.transpose(ps[:, 2 + 2 * (t % 2) + k // 4, (k % 4) * P:(k % 4 + 1) * P],
                                      h2[:, t, k * P:(k + 1) * P], ident[:])
                mm.then_inc(h2t_done, 1)
                if t >= 1:
                    logits(pe, t - 1)
            logits(pe, NT - 1)
            pe.wait_ge(both_ready, 1)
            for t in range(NT):
                for q in range(t + 1):
                    pe.matmul(ps[:, 0, t * E:(t + 1) * E], tri[:] if q == t else ones[:], both[:, q, :],
                              start=(q == 0), stop=(q == t))
            for t in range(NT):
                mm = pe.matmul(ps[:, 1, 0:E], ones[:], both[:, t, :], start=(t == 0), stop=(t == NT - 1))
            mm.then_inc(rank_done, 1)

            def turn_rows():
                for k in range(KD):
                    mm = pe.transpose(ps[:, 4, k * BLK:(k + 1) * BLK], xb[:, k:D:KD], ident[0:BLK, 0:BLK])
                mm.then_inc(xt_ps, 1)

            def expert_block(b, s, target):
                pe.wait_ge(xt_ready, b + 1)
                for k in range(KD):
                    if k % (KD // 2) == 0:
                        pe.wait_ge(gate_in[s][k // (KD // 2)], target)
                    pe.matmul(ps[0:BLK, 0, :], xT[:, k, :], gate_w[s][:, k, :], start=(k == 0), stop=(k == KD - 1))
                    if k % (KD // 2) == 0:
                        pe.wait_ge(up_in[s][k // (KD // 2)], target)
                    mm = pe.matmul(ps[BLK:2 * BLK, 1, :], xT[:, k, :], up_w[s][:, k, :],
                                   start=(k == 0), stop=(k == KD - 1))
                mm.then_inc(gu_done, 1)
                pe.wait_ge(xb_in, 16 * b + 32)
                pe.sem_inc(pe_passed, 1)
                turn_rows()
                pe.wait_ge(hb_ready, b + 1)
                pe.sem_inc(pe_passed, 1)
                for k in range(KF):
                    mm = pe.transpose(ps[:, 5, k * BLK:(k + 1) * BLK], hb[:, k:F:KF], ident[0:BLK, 0:BLK])
                mm.then_inc(ht_ps, 1)
                pe.wait_ge(ht_ready, b + 1)
                pe.wait_ge(y_evac, 2 * b + 1)
                for k in range(KF):
                    if k % (KF // 2) == 0:
                        pe.wait_ge(dn_in[s][k // (KF // 2)], target)
                    pe.matmul(ps[0:BLK, 2, :], hbT[:, k, :], down_w[s][:, k, 0:512], start=(k == 0), stop=(k == KF - 1))
                    mm = pe.matmul(ps[BLK:2 * BLK, 3, :], hbT[:, k, :], down_w[s][:, k, 512:1024],
                                   start=(k == 0), stop=(k == KF - 1))
                mm.then_inc(y_done, 1)

            pe.wait_ge(table_ready, 1)
            pe.wait_ge(xb_in, 16)
            turn_rows()
            def expert(e, s, target):
                n = pe.value_load(table[0:1, bass.ds(e, 1)], min_val=1, max_val=MAXN)
                first = pe.value_load(table[0:1, bass.ds(e + E, 1)], min_val=0, max_val=MAXB - 1)
                with pe.Fori(0, n) as j:
                    expert_block(first + j, s, target)

            with pe.Fori(0, E // SLOTS) as i:
                for s in range(SLOTS):
                    expert(SLOTS * i + s, s, 16 * i + 16)
            for e in range(E // SLOTS * SLOTS, E):
                expert(e, e % SLOTS, 16 * (e // SLOTS + 1))

        @block.scalar
        def _(act):
            for h in range(H):
                for v, (R, nq, q0, k0, nk) in enumerate(VARIANTS):
                    first_row = RPBROWS // 2 - (R - 1)
                    src = bass.AP(rpb.tensor, (h * RPBROWS + first_row) * RPBW + RPBW // 2 + k0 - q0,
                                  [[RPBW, STRIP_ROWS[v]], [-1, nq], [1, nk]])
                    dst = strips[h, STRIP_AT[v]:STRIP_AT[v] + STRIP_SIZE[v]].rearrange(
                        "(c r k) -> r c k", c=nq, r=STRIP_ROWS[v])
                    act.dma_start(dst, src).then_inc(strip_out, 16)
                if h < NT:
                    act.wait_ge(x_in[h], 16)
                    if h >= 1:
                        act.wait_ge(sq1, h)
                    nc.scalar.activation(junk, x[:, h, :], ACT.Square, accum_out=ss1[:, h:h + 1]).then_inc(sq1, 1)

            def win(c, g, half):
                kind, i = CHUNKS[c]
                if half == 0 or (kind == "conv" and g % 2 == 0):
                    return
                n = GROUP_AT[c, g]
                act.wait_ge(win_done, n + 1)
                if kind == "conv":
                    size = columns(g)[2]
                    m = 2 * i + g // 2
                    if m >= 1:
                        act.wait_ge(z_done, m)
                    nc.scalar.activation(sig[:, 0:size], ps[:, 1, 0:size], ACT.Sigmoid).then_inc(sig_ready, 1)
                elif kind == "qk":
                    sub, cols, size = columns(g)
                    nc.scalar.activation((kT if sub else qT)[:, i, cols], ps[:, n % 2, 0:size], ACT.Copy,
                                         scale=1.0 if sub else DH ** -0.5).then_inc(copy_done, 1)
                else:
                    cs = slice(2 * P * i, 2 * P * (i + 1))
                    src = ps[:, n % 2, 0:2 * P]
                    dst = vals[:, 2 * g, cs] if g < NTS else vals[:, 3 + g, cs]
                    if g < NTS - 1:
                        nc.scalar.activation(vals[0:64, 2 * g + 1, cs], src[64:128, :], ACT.Copy)
                    if 1 <= g < NTS:
                        nc.scalar.activation(vals[64:128, 2 * g - 1, cs], src[0:64, :], ACT.Copy)
                    nc.scalar.activation(dst, src, ACT.Copy).then_inc(copy_done, 1)

            def exponentials(u):
                h, t = divmod(u, NT)
                act.wait_ge(neg_done, u + 1)
                if u >= 2:
                    act.wait_ge(pt_done, u - 1)
                if t == 0 and h >= 2:
                    act.wait_ge(attn_done, h - 1)
                nc.scalar.activation(prob[:, u % 2, :], neg_s[:, u % 2, :], ACT.Exp, scale=-1.0,
                                     bias=nmax[:, u % 2:u % 2 + 1],
                                     accum_out=rsum[:, h % 2, t:t + 1]).then_inc(exp_done, 1)

            def turned(u):
                act.wait_ge(pt_done, u + 1)
                if u >= 2:
                    act.wait_ge(o_done, u - 1)
                nc.scalar.activation(probT[:, u % 2, :], ps[:, 4 + u % 2, 0:256], ACT.Copy).then_inc(ptc_done, 1)

            for what, *a in ORDER:
                if what == "win":
                    win(*a)
                elif what == "att":
                    k, = a
                    if 1 <= k <= H * NT:
                        turned(k - 1)
                    if k < H * NT:
                        exponentials(k)

            act.wait_ge(attn_done, H)
            for t in range(NT):
                if t >= 1:
                    act.wait_ge(ssa_done, t)
                nc.scalar.activation(junk[:, 0:DA], attn[:, t, :], ACT.Square,
                                     accum_out=ssa[:, t:t + 1]).then_inc(ssa_done, 1)
            for t in range(NT):
                act.wait_ge(at_done, t + 1)
                nc.scalar.activation(mT[:, 0:JC, t * P:(t + 1) * P],
                                     ps[:, 6 + t % 2, :].rearrange("p (j n) -> p j n", j=JC), ACT.Copy).then_inc(mta_done, 1)
            for t in range(NT):
                act.wait_ge(zt_done, t + 1)
                for j in range(JC):
                    nc.scalar.activation(mT[:, JC + j, t * P:(t + 1) * P], ps[:, 6 + t % 2, j * P:(j + 1) * P],
                                         ACT.Silu, scale=vec[:, V_LG + j:V_LG + j + 1],
                                         bias=vec[:, V_LB + j:V_LB + j + 1]).then_inc(silu_done, 1)
            for t in range(NT):
                act.wait_ge(x2_done, (OUT_CHUNKS - 1) * NT + t + 1)
                if t >= 1:
                    act.wait_ge(sq2, t)
                nc.scalar.activation(junk, x[:, t, :], ACT.Square, accum_out=ss2[:, t:t + 1]).then_inc(sq2, 1)
            for t in range(NT):
                act.wait_ge(h2t_done, t + 1)
                if t >= 2:
                    act.wait_ge(lg_done, t - 1)
                nc.scalar.activation(h2T[:, t % 2, :, :].rearrange("p k n -> p (k n)"),
                                     ps[:, 2 + 2 * (t % 2):4 + 2 * (t % 2), :].rearrange("p a b -> p (a b)"),
                                     ACT.Copy).then_inc(h2t_ready, 1)
            act.wait_ge(gd_ready, 1)
            nc.scalar.activation(ge[:], gd[:], ACT.Exp).then_inc(ge_ready, 1)
            act.wait_ge(dd_ready, 1)
            nc.scalar.activation(ex[:], dd[:], ACT.Exp).then_inc(ex_ready, 1)

            act.wait_ge(table_ready, 1)
            total = act.value_load(table[0:1, 3 * E - 1:3 * E], min_val=E, max_val=MAXB)

            def expert_block(b, first):
                act.wait_ge(gu_done, b + 1)
                nc.scalar.activation(sG, ps[0:BLK, 0, :], ACT.Silu).then_inc(sg_ready, 1)
                act.wait_ge(ht_ps, b + 1)
                nc.scalar.activation(hbT.rearrange("p k n -> p (k n)"), ps[:, 5, 0:KF * BLK], ACT.Copy).then_inc(ht_ready, 1)
                act.wait_ge(y_done, b + 1)
                if not first:
                    act.wait_ge(y_out, 16 * b)
                nc.scalar.activation(yb[0:BLK, :], ps[0:BLK, 2, :], ACT.Copy).then_inc(y_evac, 1)

            expert_block(0, True)
            with act.Fori(1, total) as b:
                expert_block(b, False)
            for t in range(NT):
                act.wait_ge(xf_done, t + 1)
                if t >= 1:
                    act.wait_ge(sqf, t)
                nc.scalar.activation(junk, x[:, t, :], ACT.Square, accum_out=ssf[:, t:t + 1]).then_inc(sqf, 1)

        @block.vector
        def _(dve):
            n_link = [0]

            def link(ins):
                n_link[0] += 1
                ins.then_inc(dch, 1)
                dve.wait_ge(dch, n_link[0])

            nc.vector.memset(zpad, 0.0)
            link(nc.vector.memset(zeros[:], 0.0))
            nc.vector.memset(zeros[:, 0:1], 0.0).then_inc(zeros_ready, 1)
            dve.wait_ge(vec_in, 16)
            for t in range(NT + 1):
                if t < NT:
                    dve.wait_ge(root1, t + 1)
                    if t >= 2:
                        dve.wait_ge(xps, t - 1)
                    nc.vector.tensor_scalar(xs[:, t % 2, :], x[:, t, :], r1[:, t:t + 1], None, ALU.mult).then_inc(xs_ready, 1)
                if t >= 1:
                    q = t - 1
                    dve.wait_ge(xps, q + 1)
                    src = ps[:, 2 + 2 * (q % 2):4 + 2 * (q % 2), :].rearrange("p a (k n) -> p (a k) n", n=P)
                    nc.vector.tensor_tensor(hT[:, :, q * P:(q + 1) * P], src,
                                            vec[:, V_N1:V_N1 + KD].unsqueeze(2).to_broadcast([P, KD, P]),
                                            ALU.mult).then_inc(h_ready, 1)

            def glu(c, g, half):
                kind, i = CHUNKS[c]
                if kind != "conv" or g % 2 == 0 or half == 0:
                    return
                m = 2 * i + g // 2
                dve.wait_ge(sig_ready, m + 1)
                at, R, n = (HALO, RS, LS) if g < 2 else (HALO + LS + HALO, RP, LP)
                nc.vector.tensor_tensor(zpad[:, i % 2, at:at + n].rearrange("p (r c) -> p c r", c=GRID),
                                        ps[:, 0, 0:n].rearrange("p (c r) -> p c r", r=R),
                                        sig[:, 0:n].rearrange("p (c r) -> p c r", r=R), ALU.mult).then_inc(z_done, 1)
                dve.wait_ge(z_done, m + 1)

            def tap(j, k):
                z = zpad[:, j % 2, k:k + CW]
                w = vec[:, V_CW + TAPS * j + k:V_CW + TAPS * j + k + 1]
                if k == 0:
                    link(nc.vector.tensor_scalar(conv[:, j % 2, :], z, w, vec[:, V_CB + j:V_CB + j + 1], ALU.mult, ALU.add))
                elif k < TAPS - 1:
                    link(nc.vector.scalar_tensor_tensor(conv[:, j % 2, :], z, w, conv[:, j % 2, :], ALU.mult, ALU.add))
                else:
                    for at, to, R in ((0, 0, RS), (LS + HALO, LS, RP)):
                        n = R * GRID
                        ins = nc.vector.scalar_tensor_tensor(
                            conv_out[:, j, to:to + n].rearrange("p (c r) -> p r c", r=R),
                            z[:, at:at + n].rearrange("p (r c) -> p r c", c=GRID), w,
                            conv[:, j % 2, at:at + n].rearrange("p (r c) -> p r c", c=GRID), ALU.mult, ALU.add)
                    ins.then_inc(conv_done, 1)
                    dve.wait_ge(conv_done, j + 1)

            def shifted(u):
                h, t = divmod(u, NT)
                dve.wait_ge(s_done, u + 1)
                if t == 0:
                    dve.wait_ge(bias_ready, h + 1)
                if u >= 2:
                    dve.wait_ge(exp_done, u - 1)
                nc.vector.tensor_tensor_reduce(out=neg_s[:, u % 2, :], in0=ps[:, 2 + u % 2, 0:256],
                                               in1=bias[:, h % 2, VARIANT_OF[t], :], scale=-1.0, scalar=3e38,
                                               op0=ALU.add, op1=ALU.min,
                                               accum_out=nmax[:, u % 2:u % 2 + 1]).then_inc(neg_done, 1)

            def head_out(h):
                dve.wait_ge(o_done, NT * (h + 1))
                link(nc.vector.reciprocal(rinv[:, h % 2, :], rsum[:, h % 2, :]))
                nc.vector.tensor_tensor(attn[:, :, h * DH:(h + 1) * DH],
                                        ps[:, 6 + h % 2, 0:NT * DH].rearrange("p (t d) -> p t d", t=NT),
                                        rinv[:, h % 2, :].unsqueeze(2).to_broadcast([P, NT, DH]),
                                        ALU.mult).then_inc(attn_done, 1)

            for what, *a in ORDER:
                if what == "win":
                    glu(*a)
                elif what == "tap":
                    tap(*a)
                else:
                    k, = a
                    if k < H * NT:
                        shifted(k)
                    if k >= 2 and (k - 2) % NT == NT - 1:
                        head_out((k - 2) // NT)

            for t in range(NT):
                dve.wait_ge(ct_done, t + 1)
                link(nc.vector.bn_stats(bst[:, t, :], ps[:, t, :]))
                nc.vector.bn_aggr(mv[:, t, :], bst[:, t, :]).then_inc(stat_done, 1)
            dve.wait_ge(rootl, 1)
            for t in range(NT):
                nc.vector.tensor_scalar(zn[:, t, :], ps[:, t, :], mv[:, t, 0:1], rl[:, t:t + 1],
                                        ALU.subtract, ALU.mult).then_inc(zn_ready, 1)
            dve.wait_ge(ssc_done, NT)
            nc.vector.tensor_copy(ssc[:], ps[:, 0, 0:NT]).then_inc(ssc_ready, 1)
            dve.wait_ge(roota, 1)
            dve.wait_ge(rootc, 1)
            for n in range(OUT_CHUNKS):
                for t in range(NT):
                    g = n * NT + t
                    dve.wait_ge(wout_done, g + 1)
                    xn = x[:, t, 2 * P * n:2 * P * (n + 1)]
                    link(nc.vector.scalar_tensor_tensor(xn, ps[:, 2 + g % 2, 0:2 * P], ra[:, t:t + 1], xn, ALU.mult, ALU.add))
                    nc.vector.scalar_tensor_tensor(xn, ps[:, 2 + g % 2, 2 * P:], rc[:, t:t + 1], xn,
                                                   ALU.mult, ALU.add).then_inc(x2_done, 1)
            dve.wait_ge(n2_in, 16)
            for t in range(NT):
                dve.wait_ge(root2, t + 1)
                nc.vector.scalar_tensor_tensor(h2[:, t, :], x[:, t, :], r2[:, t:t + 1], n2[:],
                                               ALU.mult, ALU.mult).then_inc(h2_ready, 1)
            dve.wait_ge(lg_done, NT)
            dve.wait_ge(small_in, 32)
            V = nc.vector

            def over(a, n):
                return a.unsqueeze(2).to_broadcast([P, NT, n])

            def same(a, shape):
                return a.unsqueeze(1).to_broadcast([P, NT, shape])

            def first_max(onehot, values, top, order, tmp, n):
                link(V.tensor_reduce(top, values, AX.X, ALU.max))
                link(V.tensor_tensor(tmp, values, over(top, n), ALU.is_equal))
                link(V.tensor_tensor(tmp, tmp, same(order, n), ALU.mult))
                link(V.tensor_reduce(t1[:], tmp, AX.X, ALU.max))
                link(V.tensor_tensor(onehot, tmp, over(t1[:], n), ALU.is_equal))

            link(V.tensor_tensor(lg[:], ps[:, 6, 0:NT * NR].rearrange("p (t n) -> p t n", t=NT), same(br[:], NR), ALU.add))
            first_max(ohg[:], lg[:, :, 0:G], g1[:], w4[:], t4[:], G)
            V.tensor_tensor(gd[:], lg[:, :, 0:G], over(g1[:], G), ALU.subtract).then_inc(gd_ready, 1)
            for g in range(G):
                lge = lg[:, :, G + g * EG:G + (g + 1) * EG]
                link(V.tensor_tensor(el[:, :, g, :], lge, over(ohg[:, :, g], EG), ALU.mult))
            link(V.tensor_tensor(es[:], el[:, :, 0, :], el[:, :, 1, :], ALU.add))
            link(V.tensor_tensor(es[:], es[:], el[:, :, 2, :], ALU.add))
            link(V.tensor_tensor(es[:], es[:], el[:, :, 3, :], ALU.add))
            first_max(oh[:, 0, :, :], es[:], m1[:], w8[:], t8[:], EG)
            link(V.scalar_tensor_tensor(es2[:], oh[:, 0, :, :], -3e38, es[:], ALU.mult, ALU.add))
            first_max(oh[:, 1, :, :], es2[:], m2[:], w8[:], t8[:], EG)
            V.tensor_tensor(dd[:], m2[:], m1[:], ALU.subtract).then_inc(dd_ready, 1)
            for j in range(2):
                for g in range(G):
                    link(V.tensor_tensor(sel[:, j, :, g * EG:(g + 1) * EG], oh[:, j, :, :], over(ohg[:, :, g], EG), ALU.mult))
            V.tensor_tensor(both, sel[:, 0, :, :], sel[:, 1, :, :], ALU.add).then_inc(both_ready, 1)
            dve.wait_ge(ge_ready, 1)
            link(V.tensor_reduce(gpi[:], ge[:], AX.X, ALU.add))
            link(V.reciprocal(gp[:], gpi[:]))
            dve.wait_ge(ex_ready, 1)
            link(V.tensor_scalar(gate2[:], ex[:], 1.0, None, ALU.add))
            link(V.reciprocal(gate1[:], gate2[:]))
            link(V.tensor_tensor(gate1[:], gate1[:], gp[:], ALU.mult))
            link(V.tensor_tensor(gate2[:], gate1[:], ex[:], ALU.mult))
            dve.wait_ge(rank_done, 1)
            link(V.tensor_copy(cnt[:], ps[:, 1, 0:E]))
            link(V.tensor_tensor(cmpb, cnt[:].unsqueeze(2).to_broadcast([P, E, MAXN - 1]),
                                 thr[:].unsqueeze(1).to_broadcast([P, E, MAXN - 1]), ALU.is_gt))
            link(V.tensor_reduce(nblk[:], cmpb, AX.X, ALU.add))
            link(V.tensor_scalar(nblk[:], nblk[:], 1.0, None, ALU.add))
            link(V.tensor_tensor_scan(endb[:], onesr[:], nblk[:], 0.0, ALU.mult, ALU.add))
            link(V.tensor_tensor(st64[:], endb[:], nblk[:], ALU.subtract))
            link(V.tensor_copy(table[0:1, 0:E], nblk[0:1, :]))
            link(V.tensor_copy(table[0:1, E:2 * E], st64[0:1, :]))
            link(V.tensor_scalar(st64[:], st64[:], float(BLK), None, ALU.mult))
            link(V.tensor_tensor(pos, ps[:, 0, 0:NT * E].rearrange("p (t e) -> p t e", t=NT), same(st64[:], E), ALU.add))
            for j in range(2):
                link(V.tensor_tensor(posd, sel[:, j, :, :], pos, ALU.mult))
                link(V.tensor_reduce(destf[:, j, :], posd, AX.X, ALU.add))
            V.tensor_copy(dest[:], destf[:]).then_inc(dest_ready, 1)
            V.memset(t1[:], 0.0).then_inc(y_evac, 1)
            V.tensor_copy(table[0:1, 2 * E:3 * E], endb[0:1, :]).then_inc(table_ready, 1)

            dve.wait_ge(table_ready, 1)
            total = dve.value_load(table[0:1, 3 * E - 1:3 * E], min_val=E, max_val=MAXB)

            def rows_in(b):
                dve.wait_ge(xt_ps, b + 1)
                nc.vector.tensor_copy(xT.rearrange("p k n -> p (k n)"), ps[:, 4, :]).then_inc(xt_ready, 1)

            def expert_block(b, first):
                dve.wait_ge(sg_ready, b + 1)
                nc.vector.tensor_tensor(hb, ps[BLK:2 * BLK, 1, :], sG, ALU.mult).then_inc(hb_ready, 1)
                rows_in(b + 1)
                dve.wait_ge(y_done, b + 1)
                if not first:
                    dve.wait_ge(y_out, 16 * b)
                nc.vector.tensor_copy(yb[BLK:2 * BLK, :], ps[BLK:2 * BLK, 3, :]).then_inc(y_evac, 1)

            rows_in(0)
            expert_block(0, True)
            with dve.Fori(1, total) as b:
                expert_block(b, False)

            dve.wait_ge(fin_in, 16)
            for t in range(NT + 1):
                if t < NT:
                    dve.wait_ge(gath_in[t % 2], 32 * (t // 2 + 1))
                    link(nc.vector.scalar_tensor_tensor(x[:, t, :], gath[:, t % 2, 0, :], gate1[:, t:t + 1], x[:, t, :],
                                                        ALU.mult, ALU.add))
                    nc.vector.scalar_tensor_tensor(x[:, t, :], gath[:, t % 2, 1, :], gate2[:, t:t + 1], x[:, t, :],
                                                   ALU.mult, ALU.add).then_inc(xf_done, 1)
                if t >= 1:
                    dve.wait_ge(rootf, t)
                    nc.vector.scalar_tensor_tensor(x[:, t - 1, :], x[:, t - 1, :], rf[:, t - 1:t], fin_g,
                                                   ALU.mult, ALU.mult).then_inc(fin_done, 1)


def kernel(x_prompt, x_sample, norm1_g, w_in, rpb, attn_out_g, conv_w, conv_b, conv_ln_g, conv_ln_b, conv_out_g,
           w_out, norm2_g, w_group, b_group, w_expert, b_expert, w_e_gate, w_e_up, w_e_down, final_g):
    import concourse.bacc as bacc
    from concourse.bass_utils import run_bass_kernel_spmd

    def by_partition(a):
        return np.ascontiguousarray(np.asarray(a).reshape(-1, P).T)

    taps = np.asarray(conv_w)[0].reshape(TAPS, JC, P).transpose(2, 1, 0).reshape(P, JC * TAPS)
    vectors = np.concatenate([by_partition(norm1_g), taps, by_partition(conv_b), by_partition(conv_ln_g),
                              by_partition(conv_ln_b), by_partition(attn_out_g), by_partition(conv_out_g)], axis=1)
    router = np.concatenate([np.asarray(w_group)[0], np.asarray(w_expert)[0].transpose(1, 0, 2).reshape(D, E)], axis=1)
    router = router.reshape(KD, P, NR).transpose(1, 0, 2).reshape(P, KD * NR)
    router_b = np.concatenate([np.asarray(b_group)[0], np.asarray(b_expert)[0].reshape(E)])
    side = (RPBW - np.shape(rpb)[3]) // 2
    arrays = {
        "x_prompt": x_prompt, "x_sample": x_sample, "w_in": w_in,
        "rpb": np.pad(np.asarray(rpb)[0], ((0, 0), (0, 0), (side, side))),
        "vectors": vectors, "w_out": w_out, "norm2": norm2_g, "router_w": router, "router_b": router_b,
        "w_gate": w_e_gate, "w_up": w_e_up, "w_down": w_e_down, "final_g": final_g,
    }
    nc = bacc.Bacc("TRN2", target_bir_lowering=False, num_devices=1)
    ins, args = {}, []
    for name, a in arrays.items():
        a = np.ascontiguousarray(a)
        ins["in_" + name] = a
        args.append(nc.dram_tensor("in_" + name, a.shape, mybir.dt.from_np(a.dtype), kind="ExternalInput").ap())
    for name, like in (("y_prompt", x_prompt), ("y_sample", x_sample)):
        args.append(nc.dram_tensor("out_" + name, np.shape(like), F32, kind="ExternalOutput").ap())
    encoder(nc, *args)
    r = run_bass_kernel_spmd(nc, [ins], core_ids=[0]).results[0]
    return r["out_y_prompt"], r["out_y_sample"]
```

```python
from contextlib import ExitStack

import numpy as np

import concourse.bass as bass
from concourse import mybir

ALU = mybir.AluOpType
ACT = mybir.ActivationFunctionType
F32 = mybir.dt.float32
F32R = mybir.dt.float32r
I32 = mybir.dt.int32
U32 = mybir.dt.uint32
AX = mybir.AxisListType

P = 128
D = 1024
KD = D // P
GRID = 64
LS, LP = 512, 256
T = LS + LP
NT = T // P
NTS = LS // P
RS, RP = LS // GRID, LP // GRID
H, DH = 8, 64
DA = H * DH
JC = (D - DA) // P
TAPS = 31
HALO = TAPS // 2
EPS = 1e-6
NEG = -1e30
G, EG = 4, 8
E = G * EG
F = 512
KF = F // P
BLK = 64
MAXB = 2 * T // BLK + E
XROWS = -(-(MAXB + 1) * BLK // P) * P
ZERO_TILES = 2
ZERO_DMAS = -(-XROWS // P // ZERO_TILES)
NR = G + E
MAXN = T // BLK
SLOTS = 3

RPBW = 127
RPBROWS = 15
VARIANTS = [(RS, 16, 0, 0, 32), (RS, 16, 16, 8, 32), (RS, 16, 48, 32, 32), (RP, 32, 0, 0, 64), (RP, 32, 32, 0, 64)]
NV = len(VARIANTS)
VARIANT_OF = [0, 1, 1, 2, 3, 4]
KEYS_AT = [0, 64, 192, 256, LS, LS]
VALUES_AT = [(0, 2), (1, 3), (3, 5), (4, 6), (7, 8), (7, 8)]
STRIP_ROWS = [2 * v[0] - 1 for v in VARIANTS]
STRIP_SIZE = [v[1] * n * v[4] for v, n in zip(VARIANTS, STRIP_ROWS)]
STRIP_AT = [sum(STRIP_SIZE[:i]) for i in range(NV)]
STRIPS = sum(STRIP_SIZE)

V_CW, V_CB = 0, JC * TAPS
V_LG, V_LB, V_GO = V_CB + JC, V_CB + 2 * JC, V_CB + 3 * JC
NVEC = V_GO + KD

CHUNKS = [("conv", 0), ("v", 0), ("v", 1), ("qk", 0), ("conv", 1), ("qk", 1), ("conv", 2), ("qk", 2), ("conv", 3), ("qk", 3)]
RUNS = 2 * len(CHUNKS)
OUT_CHUNKS = 4
BY_DVE = (3, 4, 5, 6)


def split_count(run):
    if run in BY_DVE:
        return "dve", BY_DVE.index(run) + 1
    return "pool", run + 1 - sum(q < run for q in BY_DVE)


def run_column(run):
    (kind, i), sub = CHUNKS[run // 2], run % 2
    if kind == "conv":
        return 3 * DA + P * i + (0 if sub else D - DA)
    if kind == "qk":
        return P * i + DA * sub
    return 2 * DA + 2 * P * i + P * sub


HI_LO = [(0, 0), (0, 1), (1, 0)]


def groups_of(c):
    return NT if CHUNKS[c][0] == "v" else 4


def plan():
    order = [("split", 0), ("split", 1)]
    att, side, qk_done, v_done, budget, zeroed = 0, [], 0, False, 0.0, 0

    def slot(pe_time, wins_left, attention=True):
        nonlocal att, budget
        if attention and v_done and att < (NATT if qk_done == H // 2 else 2 * NT * qk_done):
            order.append(("att", att))
            att += 1
            budget += PE_ATT - DVE_COST["att"]
            if att % NT == 0 and 2 <= att // NT + 1 < H:
                order.append(("bias", att // NT + 1))
        budget = min(budget + pe_time, 4.0)
        while side and side[0][0] in DVE_COST and budget >= DVE_COST[side[0][0]]:
            if not wins_left or side[0][0] == "tap":
                budget -= DVE_COST[side[0][0]]
                order.append(side.pop(0))
            else:
                break

    for c, (kind, i) in enumerate(CHUNKS):
        if (kind, i) in (("v", 0), ("v", 1)):
            order.append(("bias", i))
        for g in range(groups_of(c)):
            for half in range(2):
                order.append(("win", c, g, half))
                slot(2.75 if kind != "v" and g % 2 == 0 else 1.4, True)
            if kind == "conv" and g >= 2:
                budget -= 0.7
            if g % 2 == 0 and zeroed < ZERO_DMAS:
                order.append(("zero", zeroed))
                zeroed += 1
            freed = {1: (2 * c,), 3: (2 * c + 1,)}.get(g, ()) if kind != "v" else (2 * c, 2 * c + 1) if g == NT - 1 else ()
            order += [("split", run + 2) for run in freed if run + 2 < RUNS]
        if kind == "qk":
            qk_done += 1
        v_done = v_done or (kind, i) == ("v", 1)
        if kind == "conv":
            side += [("tap", i, k) for k in range(TAPS)]
            if i == JC - 1:
                side += [("wo", 0)] + [(what, t) for t in range(NT) for what in ("ln", "zn")] + [("at", u) for u in range(6)]
    while att < NATT:
        slot(TAIL_STEP, False)
    order += side + [("at", 6), ("at", 7)]
    for t in range(NT + 2):
        order += [("silu", t), ("sq", t)] if t < NT else []
        order += [("cg", t - 1)] if 1 <= t <= NT else []
        order += [("lo", t - 2)] if t >= 2 else []
        order += [("wo", 1)] if t == 1 else []
    return order + [("ssc", t) for t in range(NT)]


NATT = H * NT + 2
PE_ATT = 1.1
DVE_COST = dict(att=0.5, tap=1.08, ln=1.6, zn=1.0, wo=0, sq=0, cg=0.8, at=0.8)
TAIL_STEP = 1.4
ORDER = plan()
PIECE = {e: n for n, e in enumerate(e for e in ORDER if e[0] in ("cg", "at"))}
PIECES = len(PIECE)


def accumulation_groups():
    at, n = {}, 0
    for c in range(len(CHUNKS)):
        for g in range(groups_of(c)):
            at[c, g] = n
            n += 1
    return at


GROUP_AT = accumulation_groups()


def taken_out():
    out, copies = {}, 0
    for (c, g), n in GROUP_AT.items():
        kind, i = CHUNKS[c]
        if kind == "conv":
            out[n] = ("z" if g >= 2 else "sig", 2 * i + g % 2 + 1)
        else:
            copies += 1
            out[n] = ("copy", copies)
    return out


TAKEN_OUT = taken_out()


def copies_after(kind, i):
    c = CHUNKS.index((kind, i))
    return TAKEN_OUT[GROUP_AT[c, groups_of(c) - 1]][1]


def run_freed(run):
    c, sub = divmod(run, 2)
    return GROUP_AT[c, NT - 1 if CHUNKS[c][0] == "v" else 2 * sub + 1] + 1


def encoder(nc, x_prompt, x_sample, norm1, w_in, rpb, vectors, w_out, norm2, router_w, router_b,
            w_gate, w_up, w_down, final_g, y_prompt, y_sample):
    strips = nc.dram_tensor("strips", (H, STRIPS), F32, kind="Internal").ap()
    rows = nc.dram_tensor("rows", (XROWS, D), F32, kind="Internal").ap()

    def rows_of(x_p, x_s, t):
        if t < NTS:
            n = P // RS
            return x_s[0].rearrange("(r c) d -> c r d", c=GRID)[n * t:n * t + n]
        n = P // RP
        return x_p[0].rearrange("(r c) d -> c r d", c=GRID)[n * (t - NTS):n * (t - NTS) + n]

    with ExitStack() as ctx:
        def sb(name, shape, dt=F32):
            return ctx.enter_context(nc.sbuf_tensor(name, shape, dt))

        def sem(name):
            return ctx.enter_context(nc.semaphore(name))

        ZW = HALO + LS + HALO + LP + HALO
        CW = ZW - 2 * HALO
        with ExitStack() as early:
            def at(name, shape, dt=F32):
                return early.enter_context(nc.sbuf_tensor(name, shape, dt))[:]

            qk = at("qk", [P, 2, 4, T])
            qT, kT = qk[:, 0, :, :], qk[:, 1, :, :]
            hT = at("hT", [P, 2, KD, T], F32R)
            w_split = at("w_split", [P, 2, 2, KD, P], F32R)
            w_raw = at("w_raw", [P, 2, KD, P])
            vals = at("vals", [P, 9, DA])
            mask = at("mask", [P, NV, 256])
        x = sb("x", [P, NT, D])[:]
        with ExitStack() as middle:
            middle.enter_context(nc.sbuf_tensor("under_hT", [P, 2 * KD * T], F32R))
            wo_split, wo_raw = [], []
            for b in range(2):
                wo_split.append(middle.enter_context(nc.sbuf_tensor(f"wo_split{b}", [P, 2, KD, 2 * P], F32R))[:])
                wo_raw.append(middle.enter_context(nc.sbuf_tensor(f"wo_raw{b}", [P, KD, 2 * P], F32))[:])
        mT = hT
        ring = sb("ring", [P, 2, (2 * KD * F + KF * D)])[:]
        slot0, slot1 = ring[:, 0, :], ring[:, 1, :]
        gath = slot0.rearrange("p (t j d) -> p t j d", t=NT, j=2)

        MID = 2 * ZW + 2 * CW + JC * T + 4 * NV * 256
        big = sb("big", [P, MID + NT * DA + 3 * D])
        mid, attn, scr = big[:, 0:MID], big[:, MID:MID + NT * DA], big[:, MID + NT * DA:]
        attn = attn.rearrange("p (t n) -> p t n", t=NT)
        zpad = mid[:, 0:2 * ZW].rearrange("p (b n) -> p b n", b=2)
        conv = mid[:, 2 * ZW:2 * ZW + 2 * CW].rearrange("p (b n) -> p b n", b=2)
        o = 2 * ZW + 2 * CW
        conv_out = mid[:, o:o + JC * T].rearrange("p (j n) -> p j n", j=JC)
        zn = mid[:, 0:NT * DA].rearrange("p (t n) -> p t n", t=NT)
        sq = mid[:, o:o + NT * DA].rearrange("p (t n) -> p t n", t=NT)
        o += JC * T
        raw = mid[:, o:o + 2 * NV * 256].rearrange("p (b v n) -> p b v n", b=2, v=NV)
        bias = mid[:, o + 2 * NV * 256:].rearrange("p (b v n) -> p b v n", b=2, v=NV)
        n1 = mid[:, o + 2 * NV * 256:o + 2 * NV * 256 + D]
        attn_sq = mid[:, o:o + DA]
        h2 = mid[:, 0:NT * D].rearrange("p (t d) -> p t d", t=NT)
        h2T = mid[:, NT * D:NT * D + 2 * D].rearrange("p (b k n) -> p b k n", b=2, k=KD)
        slot2_gu, slot2_dn = big[:, (NT + 2) * D:(NT + 2) * D + 2 * KD * F], big[:, 0:KF * D]
        gus = [slot0[:, 0:2 * KD * F], slot1[:, 0:2 * KD * F], slot2_gu]
        dns = [slot0[:, 2 * KD * F:], slot1[:, 2 * KD * F:], slot2_dn]
        gate_w = [g[:, 0:KD * F].rearrange("p (k f) -> p k f", k=KD) for g in gus]
        up_w = [g[:, KD * F:].rearrange("p (k f) -> p k f", k=KD) for g in gus]
        down_w = [d.rearrange("p (k d) -> p k d", k=KF) for d in dns]
        o = KF * D
        xb = big[0:BLK, o:o + D]
        xT = big[:, o + D:o + D + KD * BLK].rearrange("p (k n) -> p k n", k=KD)
        sG = big[64:128, o + 2 * D:o + 2 * D + F]
        hb = big[0:BLK, o + 2 * D + F:o + 2 * D + 2 * F]
        hbT = big[:, o + 3 * D:o + 3 * D + KF * BLK].rearrange("p (k n) -> p k n", k=KF)
        yb = big[:, o + 3 * D + 512:o + 4 * D]
        xs = scr[:, 0:2 * D].rearrange("p (b d) -> p b d", b=2)
        junk = scr[:, 2 * D:3 * D]
        neg_s = scr[:, 0:512].rearrange("p (b n) -> p b n", b=2)
        prob = scr[:, 512:1024].rearrange("p (b n) -> p b n", b=2)
        probT = scr[:, 1024:1536].rearrange("p (b n) -> p b n", b=2)
        sig = scr[:, 1536:1536 + T]
        gained = scr[:, 1536:2560].rearrange("p (b n) -> p b n", b=2)
        n2 = sb("n2", [P, D])
        fin_g = n2[:]
        zeros = sb("zeros", [P, D])
        vec = sb("vec", [P, NVEC])
        wr = sb("wr", [P, KD, NR])
        br = sb("br", [P, NR])
        ident = sb("ident", [P, P])
        tri = sb("tri", [P, P])
        ones = sb("ones", [P, P])
        w8 = sb("w8", [P, EG])
        w4 = sb("w4", [P, G])
        thr = sb("thr", [P, MAXN - 1])
        half_neg = sb("half_neg", [P, NT])
        ss1 = sb("ss1", [P, NT]); r1 = sb("r1", [P, NT])
        ssa = sb("ssa", [P, NT]); ra = sb("ra", [P, NT])
        ssc = sb("ssc", [P, NT]); rc = sb("rc", [P, NT])
        ss2 = sb("ss2", [P, NT]); r2 = sb("r2", [P, NT])
        ssf = sb("ssf", [P, NT]); rf = sb("rf", [P, NT])
        bst = sb("bst", [P, NT, 6]); mv = sb("mv", [P, NT, 2]); rl = sb("rl", [P, NT])
        nmax = sb("nmax", [P, 2]); rsum = sb("rsum", [P, 2, NT]); rinv = sb("rinv", [P, 2, NT])
        lg = sb("lg", [P, NT, NR])
        g1 = sb("g1", [P, NT]); gd = sb("gd", [P, NT, G]); ge = sb("ge", [P, NT, G])
        gpi = sb("gpi", [P, NT]); gp = sb("gp", [P, NT])
        t4 = sb("t4", [P, NT, G]); t1 = sb("t1", [P, NT]); ohg = sb("ohg", [P, NT, G])
        es = sb("es", [P, NT, EG]); es2 = sb("es2", [P, NT, EG])
        m1 = sb("m1", [P, NT]); m2 = sb("m2", [P, NT]); t8 = sb("t8", [P, NT, EG])
        oh = sb("oh", [P, 2, NT, EG])
        dd = sb("dd", [P, NT]); ex = sb("ex", [P, NT]); gate1 = sb("gate1", [P, NT]); gate2 = sb("gate2", [P, NT])
        o = NT * D
        el = mid[:, o:o + NT * E].rearrange("p (t g e) -> p t g e", t=NT, g=G)
        sel = mid[:, o:o + 2 * NT * E].rearrange("p (j t e) -> p j t e", j=2, t=NT)
        el_cmp = mid[:, o + (6 * NT + 2) * E:o + (6 * NT + 2 + MAXN - 1) * E]
        both = mid[:, o + 2 * NT * E:o + (3 * NT + 1) * E].rearrange("p (t e) -> p t e", t=NT + 1)
        before = mid[:, o + (3 * NT + 1) * E:o + (4 * NT + 2) * E].rearrange("p (t e) -> p t e", t=NT + 1)
        pos = mid[:, o + (4 * NT + 2) * E:o + (5 * NT + 2) * E].rearrange("p (t e) -> p t e", t=NT)
        posd = mid[:, o + (5 * NT + 2) * E:o + (6 * NT + 2) * E].rearrange("p (t e) -> p t e", t=NT)
        cmpb = el_cmp[:, 0:E * (MAXN - 1)].rearrange("p (e n) -> p e n", e=E)
        cnt = sb("cnt", [P, E]); nblk = sb("nblk", [P, E])
        onesr = sb("onesr", [P, E]); endb = sb("endb", [P, E]); st64 = sb("st64", [P, E])
        destf = sb("destf", [P, 2, NT])
        dest = sb("dest", [P, 2, NT], U32)
        table = sb("table", [1, 3 * E], I32)

        ps = ctx.enter_context(nc.psum_tensor("ps", [P, 8, 512], F32))

        x_in = [sem(f"x_in{t}") for t in range(NT)]
        vec_in, small_in, n2_in, fin_in = sem("vec_in"), sem("small_in"), sem("n2_in"), sem("fin_in")
        n1_in = sem("n1_in")
        win_in = [sem(f"win_in{b}") for b in range(2)]
        wout_in = [sem(f"wout_in{b}") for b in range(2)]
        hi_done, split_done = sem("hi_done"), {"pool": sem("split_done"), "dve": sem("split_done_dve")}
        hhi_done = sem("hhi_done")
        strip_out, raw_in = sem("strip_out"), [sem("raw_in0"), sem("raw_in1")]
        zero_out = sem("zero_out")
        consts = sem("consts")
        sq1, root1, xs_ready, xps, h_ready = sem("sq1"), sem("root1"), sem("xs_ready"), sem("xps"), sem("h_ready")
        win_done = sem("win_done")
        copy_done = sem("copy_done")
        sig_ready, z_done, conv_done = sem("sig_ready"), sem("z_done"), sem("conv_done")
        bias_ready, zeros_ready, ssc_ready = sem("bias_ready"), sem("zeros_ready"), sem("ssc_ready")
        s_done, neg_done, exp_done, pt_done, ptc_done, o_done, attn_done = (
            sem("s_done"), sem("neg_done"), sem("exp_done"), sem("pt_done"), sem("ptc_done"), sem("o_done"), sem("attn_done"))
        dch = sem("dch")
        pch = sem("pch")
        ct_done, stat_done, rootl, zn_ready, zt_done, silu_done, sq_ready, ssc_done, ssa_done, rootc, roota = (
            sem("ct_done"), sem("stat_done"), sem("rootl"), sem("zn_ready"), sem("zt_done"), sem("silu_done"),
            sem("sq_ready"), sem("ssc_done"), sem("ssa_done"), sem("rootc"), sem("roota"))
        at_done = sem("at_done")
        gained_done, mhi_done, m_done, mc_done = sem("gained_done"), sem("mhi_done"), sem("m_done"), sem("mc_done")
        ohi_done, osplit_done = sem("ohi_done"), sem("osplit_done")
        wout_done, x2_done = sem("wout_done"), sem("x2_done")
        sq2, root2, h2_ready, h2t_done, h2t_ready, lg_done = (
            sem("sq2"), sem("root2"), sem("h2_ready"), sem("h2t_done"), sem("h2t_ready"), sem("lg_done"))
        gd_ready, ge_ready, both_ready, rank_done, dd_ready, ex_ready, dest_ready, table_ready = (
            sem("gd_ready"), sem("ge_ready"), sem("both_ready"), sem("rank_done"), sem("dd_ready"), sem("ex_ready"),
            sem("dest_ready"), sem("table_ready"))
        scattered = sem("scattered")
        gate_in = [[sem(f"gate_in{s}{q}") for q in range(2)] for s in range(SLOTS)]
        up_in = [[sem(f"up_in{s}{q}") for q in range(2)] for s in range(SLOTS)]
        dn_in = [[sem(f"dn_in{s}{q}") for q in range(2)] for s in range(SLOTS)]
        xb_in, xt_ps, xt_ready, gu_done, sg_ready, hb_ready, ht_ps, ht_ready, y_done, y_evac, y_out = (
            sem("xb_in"), sem("xt_ps"), sem("xt_ready"), sem("gu_done"), sem("sg_ready"), sem("hb_ready"),
            sem("ht_ps"), sem("ht_ready"), sem("y_done"), sem("y_evac"), sem("y_out"))
        pe_passed, pool_passed = sem("pe_passed"), sem("pool_passed")
        gath_in = [sem(f"gath_in{t}") for t in range(NT)]
        xf_done, sqf, rootf, fin_done, out_done = sem("xf_done"), sem("sqf"), sem("rootf"), sem("fin_done"), sem("out_done")

        block = ctx.enter_context(nc.Block())

        def columns(g):
            return g // 2, (slice(LS, T) if g % 2 else slice(0, LS)), (LP if g % 2 else LS)

        def wait_split(engine, run):
            who, count = split_count(run)
            engine.wait_ge(split_done[who], count)

        def place_of(piece):
            what, n = piece
            if what == "cg":
                return JC, KD, n * P, (n + 1) * P
            return n // 2, n // 2 + 1, n % 2 * 3 * P, (n % 2 + 1) * 3 * P

        def fp32(a):
            return a.bitcast(F32)

        def logits(pe, t):
            pe.wait_ge(h2t_ready, t + 1)
            for k in range(KD):
                mm = pe.matmul(ps[:, 6, t * NR:(t + 1) * NR], h2T[:, t % 2, k, :], wr[:, k, :],
                               start=(k == 0), stop=(k == KD - 1))
            mm.then_inc(lg_done, 1)

        @block.sync
        def _(sp):
            def load_win(run):
                if run >= 2:
                    wait_split(sp, run - 2)
                col = run_column(run)
                sp.dma_start(w_raw[:, run % 2], w_in[0, :, col:col + P].rearrange("(k p) n -> p k n", p=P)
                             ).then_inc(win_in[run % 2], 16)

            def write_strips(heads):
                for h in heads:
                    for v, (R, nq, q0, k0, nk) in enumerate(VARIANTS):
                        first_row = RPBROWS // 2 - (R - 1)
                        src = bass.AP(rpb.tensor, (h * RPBROWS + first_row) * RPBW + RPBW // 2 + k0 - q0,
                                      [[RPBW, STRIP_ROWS[v]], [-1, nq], [1, nk]])
                        dst = strips[h, STRIP_AT[v]:STRIP_AT[v] + STRIP_SIZE[v]].rearrange(
                            "(c r k) -> r c k", c=nq, r=STRIP_ROWS[v])
                        sp.dma_start(dst, src).then_inc(strip_out, 16)

            def load_raw(h):
                for v, (R, nq, q0, k0, nk) in enumerate(VARIANTS):
                    src = bass.AP(strips.tensor, h * STRIPS + STRIP_AT[v] + (R - 1) * nk,
                                  [[STRIP_ROWS[v] * nk, nq], [-nk, R], [1, R * nk]])
                    sp.dma_start(raw[:, h % 2, v, :], src).then_inc(raw_in[h % 2], 16)

            for t in range(NT):
                sp.dma_start(x[:, t, :], rows_of(x_prompt, x_sample, t)).then_inc(x_in[t], 16)
                if t == 0:
                    sp.dma_start(n1, bass.AP(norm1.tensor, 0, [[0, P], [1, D]])).then_inc(n1_in, 16)
            load_win(0)
            load_win(1)
            sp.dma_start(vec[:], vectors).then_inc(vec_in, 16)
            write_strips(range(H // 2))
            load_win(2)
            load_win(3)
            write_strips(range(H // 2, H))
            sp.dma_start(wr[:], router_w.rearrange("p (k n) -> p k n", k=KD)).then_inc(small_in, 16)
            sp.dma_start(br[:], bass.AP(router_b.tensor, 0, [[0, P], [1, NR]])).then_inc(small_in, 16)
            sp.dma_start(n2[:], bass.AP(norm2.tensor, 0, [[0, P], [1, D]])).then_inc(n2_in, 16)
            sp.wait_ge(strip_out, 16 * H * NV)
            load_raw(0)
            load_raw(1)
            for what, *a in ORDER:
                if what == "split" and 4 <= a[0] + 2 < RUNS:
                    load_win(a[0] + 2)
                elif what == "bias" and a[0] + 2 < H:
                    sp.wait_ge(bias_ready, a[0] + 1)
                    load_raw(a[0] + 2)
            wait_split(sp, RUNS - 1)
            for n in range(OUT_CHUNKS):
                if n == 1:
                    sp.wait_ge(bias_ready, H)
                    sp.wait_ge(o_done, H * NT)
                if n >= 2:
                    sp.wait_ge(osplit_done, n - 1)
                sp.dma_start(wo_raw[n % 2], w_out[0, :, 2 * P * n:2 * P * (n + 1)].rearrange(
                    "(k p) n -> p k n", p=P)).then_inc(wout_in[n % 2], 16)
                if n == 1:
                    sp.wait_ge(s_done, H * NT)
                    for t in range(NT):
                        sp.dma_start(x[:, t, :], rows_of(x_prompt, x_sample, t)).then_inc(x_in[t], 16)

            def in_order(s):
                for q in range(2):
                    ks = slice(q * KD // 2, (q + 1) * KD // 2)
                    yield gate_in[s][q], gate_w[s], w_gate, ks
                    yield up_in[s][q], up_w[s], w_up, ks
                for q in range(2):
                    yield dn_in[s][q], down_w[s], w_down, slice(q * KF // 2, (q + 1) * KF // 2)

            def load(e, landed, to, w, ks):
                sp.dma_start(to[:, ks, :], w[0, bass.ds(e, 1)].rearrange(
                    "e (p k) f -> p (e k) f", p=P)[:, ks, :]).then_inc(landed, 16)

            def load_gate_up(e, s):
                for l in list(in_order(s))[0:4]:
                    load(e, *l)

            def load_down(e, s):
                for l in list(in_order(s))[4:]:
                    load(e, *l)

            def load_expert(i, s):
                e = SLOTS * i + s
                end = sp.value_load(table[0:1, bass.ds(e + (2 * E - SLOTS), 1)], min_val=1, max_val=MAXB)
                before = list(in_order((s - 1) % SLOTS))[-2:]
                loads = list(in_order(s))
                for n, l in enumerate(loads):
                    if n < 2:
                        sp.wait_ge(before[n][0], 16 * i + (16 if s else 0))
                    else:
                        sp.wait_ge(loads[n - 2][0], 16 * i + 16)
                    if n == 0:
                        sp.wait_ge(gu_done, end)
                    elif n == 4:
                        sp.wait_ge(y_done, end)
                    load(e, *l)

            sp.wait_ge(wout_done, 1)
            sp.wait_ge(ssa_done, NT)
            load_gate_up(2, 2)
            sp.wait_ge(wout_done, NT * OUT_CHUNKS)
            for e in range(2):
                load_gate_up(e, e)
                load_down(e, e)
            sp.wait_ge(h2_ready, NT)
            sp.dma_start(fin_g, bass.AP(final_g.tensor, 0, [[0, P], [1, D]])).then_inc(fin_in, 16)
            sp.wait_ge(scattered, 16 * 2 * NT)
            sp.wait_ge(xb_in, 16)
            load_down(2, 2)
            sp.wait_ge(table_ready, 1)
            with sp.Fori(1, E // SLOTS) as i:
                for s in range(SLOTS):
                    load_expert(i, s)
            for e in range(E // SLOTS * SLOTS, E):
                load_expert(e // SLOTS, e % SLOTS)
            for t in range(NT):
                sp.wait_ge(fin_done, t + 1)
                sp.dma_start(rows_of(y_prompt, y_sample, t), x[:, t, :]).then_inc(out_done, 16)
            sp.wait_ge(out_done, 16 * NT)

        @block.gpsimd
        def _(pool):
            n_link = [0]

            def link(ins):
                n_link[0] += 1
                ins.then_inc(pch, 1)
                pool.wait_ge(pch, n_link[0])

            link(nc.gpsimd.memset(ident[:], 0.0))
            link(nc.gpsimd.memset(tri[:], 0.0))
            nc.gpsimd.memset(half_neg[:], -0.5).then_inc(consts, 1)
            nc.gpsimd.affine_select(out=ident[:], in_=ident[:], compare_op=ALU.not_equal, fill=1.0, base=0,
                                    pattern=[[-1, P]], channel_multiplier=1).then_inc(consts, 1)
            nc.gpsimd.affine_select(out=tri[:], in_=tri[:], compare_op=ALU.is_ge, fill=1.0, base=0,
                                    pattern=[[-1, P]], channel_multiplier=1).then_inc(consts, 1)
            nc.gpsimd.memset(ones[:], 1.0).then_inc(consts, 1)
            nc.gpsimd.iota(w8[:], [[-1, EG]], base=EG, channel_multiplier=0,
                           allow_small_or_imprecise_dtypes=True).then_inc(consts, 1)
            nc.gpsimd.iota(w4[:], [[-1, G]], base=G, channel_multiplier=0,
                           allow_small_or_imprecise_dtypes=True).then_inc(consts, 1)
            nc.gpsimd.iota(thr[:], [[BLK, MAXN - 1]], base=BLK, channel_multiplier=0,
                           allow_small_or_imprecise_dtypes=True).then_inc(consts, 1)
            nc.gpsimd.memset(onesr[:], 1.0).then_inc(consts, 1)

            def root(out, in_, scale, ready, n):
                link(nc.gpsimd.tensor_scalar(out, in_, scale, EPS, ALU.mult, ALU.add))
                nc.gpsimd.tensor_tensor(out, out, half_neg[:, 0:n], ALU.pow).then_inc(ready, 1)

            link(nc.gpsimd.memset(mask[:], 0.0))
            for v, (R, nq, q0, k0, nk) in enumerate(VARIANTS):
                lo = mask[:, v, 0:(48 - k0) * R] if k0 + nk > 48 else mask[:, v, :]
                n = min(nk, 48 - k0)
                lo = lo.rearrange("p (c r) -> p c r", r=R)
                link(nc.gpsimd.affine_select(out=lo, in_=lo, compare_op=ALU.is_ge, fill=NEG,
                                             base=R * (k0 - q0 + 8) + R - 1, pattern=[[R, n], [0, R]],
                                             channel_multiplier=-1))
                s = max(0, 16 - k0)
                hi = mask[:, v, s * R:].rearrange("p (c r) -> p c r", r=R)
                link(nc.gpsimd.affine_select(out=hi, in_=hi, compare_op=ALU.is_ge, fill=NEG,
                                             base=R * (q0 - k0 + 7 - s), pattern=[[-R, nk - s], [0, R]],
                                             channel_multiplier=1))
            pool.wait_ge(consts, 1)
            for t in range(NT):
                pool.wait_ge(sq1, t + 1)
                root(r1[:, t:t + 1], ss1[:, t:t + 1], 1.0 / D, root1, 1)

            def lo_of_run(run):
                pool.wait_ge(hi_done, run + 1)
                hi, lo = w_split[:, run % 2, 0], w_split[:, run % 2, 1]
                nc.gpsimd.tensor_tensor(lo, w_raw[:, run % 2], fp32(hi), ALU.subtract).then_inc(split_done["pool"], 1)

            def bias_of(h):
                b = h % 2
                pool.wait_ge(raw_in[b], 16 * NV * (h // 2 + 1))
                if h >= 2:
                    pool.wait_ge(neg_done, NT * (h - 1))
                for v0, v1, R in ((0, 3, RS), (3, 5, RP)):
                    dst = bias[:, b, v0:v1, :].rearrange("p v (c r) -> p v c r", r=R)
                    ins = nc.gpsimd.tensor_tensor(
                        dst, raw[:, b, v0:v1, :].rearrange("p v (r c) -> p v c r", r=R),
                        mask[:, v0:v1, :].rearrange("p v (c r) -> p v c r", r=R), ALU.add)
                ins.then_inc(bias_ready, 1)

            def zero_rows(n):
                if n == 0:
                    pool.wait_ge(zeros_ready, 1)
                first, last = ZERO_TILES * n, min(ZERO_TILES * (n + 1), XROWS // P)
                pool.dma_start(rows[P * first:P * last, :].rearrange("(n p) d -> p n d", p=P),
                               zeros[:].unsqueeze(1).to_broadcast([P, last - first, D])).then_inc(zero_out, 16)

            def lo_of_m(piece):
                n = PIECE[piece]
                pool.wait_ge(mhi_done, n + 1)
                j, k, t0, t1 = place_of(piece)
                m = gained[:, n % 2, 0:(k - j) * (t1 - t0)].rearrange("p (j n) -> p j n", j=k - j)
                nc.gpsimd.tensor_tensor(mT[:, 1, j:k, t0:t1], m, fp32(mT[:, 0, j:k, t0:t1]), ALU.subtract).then_inc(m_done, 1)

            def lo_of_w_out(n):
                pool.wait_ge(ohi_done, n + 1)
                nc.gpsimd.tensor_tensor(wo_split[n % 2][:, 1], wo_raw[n % 2], fp32(wo_split[n % 2][:, 0]),
                                        ALU.subtract).then_inc(osplit_done, 1)

            pool.wait_ge(xs_ready, NT)
            for what, *a in ORDER:
                if what == "split" and a[0] not in BY_DVE:
                    lo_of_run(*a)
                elif what == "bias":
                    bias_of(*a)
                elif what == "zero":
                    zero_rows(*a)
                elif what == "ln":
                    t, = a
                    pool.wait_ge(stat_done, t + 1)
                    root(rl[:, t:t + 1], mv[:, t, 1:2], 1.0, rootl, 1)
                elif what == "sq":
                    t, = a
                    pool.wait_ge(silu_done, JC * (t + 1))
                    pool.wait_ge(ct_done, NT)
                    nc.gpsimd.tensor_tensor(sq[:, t, :], zn[:, t, :], zn[:, t, :], ALU.mult).then_inc(sq_ready, 1)
                elif what == "at":
                    lo_of_m((what, *a))
                elif what == "wo":
                    lo_of_w_out(*a)
            pool.wait_ge(ssa_done, NT)
            root(ra[:], ssa[:], 1.0 / DA, roota, NT)
            pool.wait_ge(ssc_ready, 1)
            root(rc[:], ssc[:], 1.0 / DA, rootc, NT)
            for n in range(2, OUT_CHUNKS):
                lo_of_w_out(n)
            for t in range(NT):
                pool.wait_ge(sq2, t + 1)
                root(r2[:, t:t + 1], ss2[:, t:t + 1], 1.0 / D, root2, 1)

            pool.wait_ge(zero_out, 16 * ZERO_DMAS)
            pool.wait_ge(dest_ready, 1)
            for t in range(NT):
                for j in range(2):
                    pool.indirect_dma_start(
                        out=rows, out_offset=bass.IndirectOffsetOnAxis(ap=dest[:, j, t:t + 1], axis=0),
                        in_=h2[:, t, :], in_offset=None).then_inc(scattered, 16)
            pool.wait_ge(scattered, 16 * 2 * NT)
            pool.wait_ge(table_ready, 1)
            total = pool.value_load(table[0:1, 3 * E - 1:3 * E], min_val=E, max_val=MAXB)

            def load_rows(b):
                pool.dma_start(xb, rows[bass.ds(b * BLK, BLK), :]).then_inc(xb_in, 16)

            load_rows(0)
            with pool.Fori(0, total) as b:
                pool.wait_ge(xt_ps, b + 1)
                load_rows(b + 1)
                pool.wait_ge(y_evac, 2 * b + 3)
                pool.dma_start(rows[bass.ds(b * BLK, BLK), :].rearrange("p (h c) -> h p c", h=2), yb).then_inc(y_out, 16)
            pool.wait_ge(y_out, 16 * total)
            pool.wait_ge(xb_in, 16 * total + 16)
            pool.sem_inc(pool_passed, 1)
            for t in range(NT):
                for j in range(2):
                    pool.indirect_dma_start(
                        out=gath[:, t, j, :], out_offset=None, in_=rows,
                        in_offset=bass.IndirectOffsetOnAxis(ap=dest[:, j, t:t + 1], axis=0)).then_inc(gath_in[t], 16)
            for t in range(NT):
                pool.wait_ge(sqf, t + 1)
                root(rf[:, t:t + 1], ssf[:, t:t + 1], 1.0 / D, rootf, 1)

        @block.tensor
        def _(pe):
            pe.wait_ge(consts, 8)
            for t in range(NT):
                pe.wait_ge(xs_ready, t + 1)
                if t >= 2:
                    pe.wait_ge(h_ready, t - 1)
                for k in range(KD):
                    mm = pe.transpose(ps[:, 2 + 2 * (t % 2) + k // 4, (k % 4) * P:(k % 4 + 1) * P],
                                      xs[:, t % 2, k * P:(k + 1) * P], ident[:])
                mm.then_inc(xps, 1)
            pe.wait_ge(h_ready, NT)

            def win(c, g, half):
                kind, i = CHUNKS[c]
                n = GROUP_AT[c, g]
                if half == 0:
                    if kind == "v":
                        wait_split(pe, 2 * c)
                        wait_split(pe, 2 * c + 1)
                    else:
                        wait_split(pe, 2 * c + g // 2)
                    if n >= 2:
                        who, count = TAKEN_OUT[n - 2]
                        pe.wait_ge({"z": z_done, "sig": sig_ready, "copy": copy_done}[who], count)
                for k in range(4 * half, 4 * half + 4):
                    for m, (hi_w, hi_h) in enumerate(HI_LO):
                        flags = dict(start=(k == 0 and m == 0), stop=(k == KD - 1 and m == 2))
                        if kind == "v":
                            mm = pe.matmul(ps[:, n % 2, 0:2 * P], hT[:, hi_h, k, g * P:(g + 1) * P],
                                           w_split[:, :, hi_w, k, :], **flags)
                        else:
                            sub, cols, size = columns(g)
                            mm = pe.matmul(ps[:, n % 2, 0:size], w_split[:, sub, hi_w, k, :], hT[:, hi_h, k, cols], **flags)
                if half:
                    mm.then_inc(win_done, 1)

            def scores(u):
                h, t = divmod(u, NT)
                p0 = (h % 2) * DH
                if t == 0:
                    pe.wait_ge(copy_done, copies_after("qk", h // 2))
                if u >= 2:
                    pe.wait_ge(neg_done, u - 1)
                pe.matmul(ps[:, 2 + u % 2, 0:256], qT[p0:p0 + DH, h // 2, t * P:(t + 1) * P],
                          kT[p0:p0 + DH, h // 2, KEYS_AT[t]:KEYS_AT[t] + 256], start=True, stop=True).then_inc(s_done, 1)

            def turn(u):
                pe.wait_ge(exp_done, u + 1)
                if u >= 2:
                    pe.wait_ge(ptc_done, u - 1)
                for c in range(2):
                    mm = pe.transpose(ps[:, 4 + u % 2, c * P:(c + 1) * P], prob[:, u % 2, c * P:(c + 1) * P], ident[:])
                mm.then_inc(pt_done, 1)

            def values(u):
                h, t = divmod(u, NT)
                pe.wait_ge(ptc_done, u + 1)
                if u == 0:
                    pe.wait_ge(copy_done, copies_after("v", 1))
                if t == 0 and h >= 2:
                    pe.wait_ge(attn_done, h - 1)
                for c in range(2):
                    mm = pe.matmul(ps[:, 6 + h % 2, t * DH:(t + 1) * DH], probT[:, u % 2, c * P:(c + 1) * P],
                                   vals[:, VALUES_AT[t][c], h * DH:(h + 1) * DH], start=(c == 0), stop=(c == 1))
                mm.then_inc(o_done, 1)

            def turn_conv(t):
                if t == 0:
                    pe.wait_ge(conv_done, JC)
                    pe.wait_ge(copy_done, copies_after("qk", H // 2 - 1))
                else:
                    pe.wait_ge(zn_ready, t)
                for j in range(JC):
                    mm = pe.transpose(ps[:, 0, j * P:(j + 1) * P], conv_out[:, j, t * P:(t + 1) * P], ident[:])
                mm.then_inc(ct_done, 1)

            def turn_back(t):
                if t < 2:
                    pe.wait_ge(gained_done, PIECE["at", 6 + t] + 1)
                else:
                    pe.wait_ge(silu_done, JC * (t - 1))
                for j in range(JC):
                    mm = pe.transpose(ps[:, t % 2, j * P:(j + 1) * P], zn[:, t, j * P:(j + 1) * P], ident[:])
                mm.then_inc(zt_done, 1)

            def sum_squares(t):
                if t == 0:
                    pe.wait_ge(gained_done, PIECES)
                pe.wait_ge(sq_ready, t + 1)
                for j in range(JC):
                    mm = pe.matmul(ps[:, 0, t:t + 1], sq[:, t, j * P:(j + 1) * P], ones[:, 0:1],
                                   start=(j == 0), stop=(j == JC - 1))
                mm.then_inc(ssc_done, 1)

            def turn_attention(u):
                j = u // 2
                if u == 0:
                    pe.wait_ge(zn_ready, NT)
                if u % 2 == 0:
                    pe.wait_ge(attn_done, 2 * j + 2)
                if u >= 2:
                    pe.wait_ge(gained_done, PIECE["at", u - 2] + 1)
                for q in range(3):
                    mm = pe.transpose(ps[:, u % 2, q * P:(q + 1) * P],
                                      attn[:, u % 2 * 3 + q, j * P:(j + 1) * P], ident[:])
                mm.then_inc(at_done, 1)

            for what, *a in ORDER:
                if what == "win":
                    win(*a)
                elif what == "att":
                    k, = a
                    if k < H * NT:
                        scores(k)
                    if 1 <= k <= H * NT:
                        turn(k - 1)
                    if k >= 2:
                        values(k - 2)
                elif what == "ln":
                    turn_conv(*a)
                elif what == "silu":
                    turn_back(*a)
                elif what == "ssc":
                    sum_squares(*a)
                elif what == "at":
                    turn_attention(*a)

            for n in range(OUT_CHUNKS):
                pe.wait_ge(osplit_done, n + 1)
                for t in range(NT):
                    g = n * NT + t
                    if g == 0:
                        pe.wait_ge(m_done, 2 * JC)
                        pe.wait_ge(mc_done, NT)
                    if g >= 2:
                        pe.wait_ge(x2_done, g - 1)
                    for k in range(KD):
                        part = k // JC
                        for m, (hi_w, hi_m) in enumerate(HI_LO):
                            mm = pe.matmul(ps[:, 2 + g % 2, part * 2 * P:(part + 1) * 2 * P],
                                           mT[:, hi_m, k, t * P:(t + 1) * P], wo_split[n % 2][:, hi_w, k, :],
                                           start=(k % JC == 0 and m == 0), stop=(k % JC == JC - 1 and m == 2))
                    mm.then_inc(wout_done, 1)
            pe.wait_ge(x2_done, OUT_CHUNKS * NT)
            for t in range(NT):
                pe.wait_ge(h2_ready, t + 1)
                if t >= 2:
                    pe.wait_ge(h2t_ready, t - 1)
                for k in range(KD):
                    mm = pe.transpose(ps[:, 2 + 2 * (t % 2) + k // 4, (k % 4) * P:(k % 4 + 1) * P],
                                      h2[:, t, k * P:(k + 1) * P], ident[:])
                mm.then_inc(h2t_done, 1)
                if t >= 1:
                    logits(pe, t - 1)
            logits(pe, NT - 1)
            pe.wait_ge(both_ready, 1)
            out = ps[:, 0, 0:(NT + 1) * E]
            pe.matmul(out, ones[:], before.rearrange("p t e -> p (t e)"), start=True, stop=False)
            pe.matmul(out, tri[:], both.rearrange("p t e -> p (t e)"), start=False, stop=True).then_inc(rank_done, 1)

            def turn_rows():
                for k in range(KD):
                    mm = pe.transpose(ps[:, 4, k * BLK:(k + 1) * BLK], xb[:, k:D:KD], ident[0:BLK, 0:BLK])
                mm.then_inc(xt_ps, 1)

            def expert_block(b, s, target):
                pe.wait_ge(xt_ready, b + 1)
                for k in range(KD):
                    if k % (KD // 2) == 0:
                        pe.wait_ge(gate_in[s][k // (KD // 2)], target)
                    pe.matmul(ps[0:BLK, 0, :], xT[:, k, :], gate_w[s][:, k, :], start=(k == 0), stop=(k == KD - 1))
                    if k % (KD // 2) == 0:
                        pe.wait_ge(up_in[s][k // (KD // 2)], target)
                    mm = pe.matmul(ps[BLK:2 * BLK, 1, :], xT[:, k, :], up_w[s][:, k, :],
                                   start=(k == 0), stop=(k == KD - 1))
                mm.then_inc(gu_done, 1)
                pe.wait_ge(xb_in, 16 * b + 32)
                pe.sem_inc(pe_passed, 1)
                turn_rows()
                pe.wait_ge(hb_ready, b + 1)
                pe.sem_inc(pe_passed, 1)
                for k in range(KF):
                    mm = pe.transpose(ps[:, 5, k * BLK:(k + 1) * BLK], hb[:, k:F:KF], ident[0:BLK, 0:BLK])
                mm.then_inc(ht_ps, 1)
                pe.wait_ge(ht_ready, b + 1)
                pe.wait_ge(y_evac, 2 * b + 1)
                for k in range(KF):
                    if k % (KF // 2) == 0:
                        pe.wait_ge(dn_in[s][k // (KF // 2)], target)
                    pe.matmul(ps[0:BLK, 2, :], hbT[:, k, :], down_w[s][:, k, 0:512], start=(k == 0), stop=(k == KF - 1))
                    mm = pe.matmul(ps[BLK:2 * BLK, 3, :], hbT[:, k, :], down_w[s][:, k, 512:1024],
                                   start=(k == 0), stop=(k == KF - 1))
                mm.then_inc(y_done, 1)

            pe.wait_ge(table_ready, 1)
            pe.wait_ge(xb_in, 16)
            turn_rows()
            def expert(e, s, target):
                n = pe.value_load(table[0:1, bass.ds(e, 1)], min_val=1, max_val=MAXN)
                first = pe.value_load(table[0:1, bass.ds(e + E, 1)], min_val=0, max_val=MAXB - 1)
                with pe.Fori(0, n) as j:
                    expert_block(first + j, s, target)

            with pe.Fori(0, E // SLOTS) as i:
                for s in range(SLOTS):
                    expert(SLOTS * i + s, s, 16 * i + 16)
            for e in range(E // SLOTS * SLOTS, E):
                expert(e, e % SLOTS, 16 * (e // SLOTS + 1))

        @block.scalar
        def _(act):
            def hi_of_run(run):
                act.wait_ge(win_in[run % 2], 16 * (run // 2 + 1))
                if run >= 2:
                    act.wait_ge(win_done, run_freed(run - 2))
                nc.scalar.activation(w_split[:, run % 2, 0], w_raw[:, run % 2], ACT.Copy).then_inc(hi_done, 1)

            def hi_of_h(t):
                act.wait_ge(xps, t + 1)
                src = ps[:, 2 + 2 * (t % 2):4 + 2 * (t % 2), :].rearrange("p a (k n) -> p (a k) n", n=P)
                nc.scalar.activation(hT[:, 0, :, t * P:(t + 1) * P], src, ACT.Copy).then_inc(hhi_done, 1)

            for h in range(NT):
                act.wait_ge(x_in[h], 16)
                if h >= 1:
                    act.wait_ge(sq1, h)
                nc.scalar.activation(junk, x[:, h, :], ACT.Square, accum_out=ss1[:, h:h + 1]).then_inc(sq1, 1)
                if h >= 1:
                    hi_of_h(h - 1)
                if h >= NT - 2:
                    hi_of_run(h - (NT - 2))
            hi_of_h(NT - 1)

            def win(c, g, half):
                kind, i = CHUNKS[c]
                if half == 0 or (kind == "conv" and g >= 2):
                    return
                n = GROUP_AT[c, g]
                act.wait_ge(win_done, n + 1)
                if kind == "conv":
                    _, cols, size = columns(g)
                    if g == 0 and i:
                        act.wait_ge(z_done, 2 * i)
                    nc.scalar.activation(sig[:, cols], ps[:, n % 2, 0:size], ACT.Sigmoid).then_inc(sig_ready, 1)
                elif kind == "qk":
                    sub, cols, size = columns(g)
                    nc.scalar.activation((kT if sub else qT)[:, i, cols], ps[:, n % 2, 0:size], ACT.Copy,
                                         scale=1.0 if sub else DH ** -0.5).then_inc(copy_done, 1)
                else:
                    cs = slice(2 * P * i, 2 * P * (i + 1))
                    src = ps[:, n % 2, 0:2 * P]
                    dst = vals[:, 2 * g, cs] if g < NTS else vals[:, 3 + g, cs]
                    if g < NTS - 1:
                        nc.scalar.activation(vals[0:64, 2 * g + 1, cs], src[64:128, :], ACT.Copy)
                    if 1 <= g < NTS:
                        nc.scalar.activation(vals[64:128, 2 * g - 1, cs], src[0:64, :], ACT.Copy)
                    nc.scalar.activation(dst, src, ACT.Copy).then_inc(copy_done, 1)

            def exponentials(u):
                h, t = divmod(u, NT)
                act.wait_ge(neg_done, u + 1)
                if u >= 2:
                    act.wait_ge(pt_done, u - 1)
                if t == 0 and h >= 2:
                    act.wait_ge(attn_done, h - 1)
                nc.scalar.activation(prob[:, u % 2, :], neg_s[:, u % 2, :], ACT.Exp, scale=-1.0,
                                     bias=nmax[:, u % 2:u % 2 + 1],
                                     accum_out=rsum[:, h % 2, t:t + 1]).then_inc(exp_done, 1)

            def turned(u):
                act.wait_ge(pt_done, u + 1)
                if u >= 2:
                    act.wait_ge(o_done, u - 1)
                nc.scalar.activation(probT[:, u % 2, :], ps[:, 4 + u % 2, 0:256], ACT.Copy).then_inc(ptc_done, 1)

            def swish(t):
                act.wait_ge(zt_done, t + 1)
                for j in range(JC):
                    nc.scalar.activation(zn[:, t, j * P:(j + 1) * P], ps[:, t % 2, j * P:(j + 1) * P],
                                         ACT.Silu, scale=vec[:, V_LG + j:V_LG + j + 1],
                                         bias=vec[:, V_LB + j:V_LB + j + 1]).then_inc(silu_done, 1)

            def hi_of_m(piece):
                n = PIECE[piece]
                if n == 0:
                    act.wait_ge(win_done, len(GROUP_AT))
                act.wait_ge(gained_done, n + 1)
                j, k, t0, t1 = place_of(piece)
                m = gained[:, n % 2, 0:(k - j) * (t1 - t0)].rearrange("p (j n) -> p j n", j=k - j)
                nc.scalar.activation(mT[:, 0, j:k, t0:t1], m, ACT.Copy).then_inc(mhi_done, 1)

            def hi_of_w_out(n):
                act.wait_ge(wout_in[n % 2], 16 * (n // 2 + 1))
                if n == 0:
                    act.wait_ge(win_done, len(GROUP_AT))
                elif n >= 2:
                    act.wait_ge(wout_done, NT * (n - 1))
                nc.scalar.activation(wo_split[n % 2][:, 0], wo_raw[n % 2], ACT.Copy).then_inc(ohi_done, 1)

            for what, *a in ORDER:
                if what == "win":
                    win(*a)
                elif what == "split" and a[0] >= 2:
                    hi_of_run(*a)
                elif what == "att":
                    k, = a
                    if k < H * NT:
                        exponentials(k)
                    if 1 <= k <= H * NT:
                        turned(k - 1)
                elif what == "silu":
                    swish(*a)
                elif what in ("cg", "at"):
                    hi_of_m((what, *a))
                elif what == "wo":
                    hi_of_w_out(*a)
            for t in range(NT):
                if t >= 1:
                    act.wait_ge(ssa_done, t)
                nc.scalar.activation(attn_sq, attn[:, t, :], ACT.Square, accum_out=ssa[:, t:t + 1]).then_inc(ssa_done, 1)
            for n in range(2, OUT_CHUNKS):
                hi_of_w_out(n)
            for t in range(NT):
                act.wait_ge(x2_done, (OUT_CHUNKS - 1) * NT + t + 1)
                if t >= 1:
                    act.wait_ge(sq2, t)
                nc.scalar.activation(junk, x[:, t, :], ACT.Square, accum_out=ss2[:, t:t + 1]).then_inc(sq2, 1)
            for t in range(NT):
                act.wait_ge(h2t_done, t + 1)
                if t >= 2:
                    act.wait_ge(lg_done, t - 1)
                nc.scalar.activation(h2T[:, t % 2, :, :].rearrange("p k n -> p (k n)"),
                                     ps[:, 2 + 2 * (t % 2):4 + 2 * (t % 2), :].rearrange("p a b -> p (a b)"),
                                     ACT.Copy).then_inc(h2t_ready, 1)
            act.wait_ge(gd_ready, 1)
            nc.scalar.activation(ge[:], gd[:], ACT.Exp).then_inc(ge_ready, 1)
            act.wait_ge(dd_ready, 1)
            nc.scalar.activation(ex[:], dd[:], ACT.Exp).then_inc(ex_ready, 1)

            act.wait_ge(table_ready, 1)
            total = act.value_load(table[0:1, 3 * E - 1:3 * E], min_val=E, max_val=MAXB)

            def expert_block(b, first):
                act.wait_ge(gu_done, b + 1)
                nc.scalar.activation(sG, ps[0:BLK, 0, :], ACT.Silu).then_inc(sg_ready, 1)
                act.wait_ge(ht_ps, b + 1)
                nc.scalar.activation(hbT.rearrange("p k n -> p (k n)"), ps[:, 5, 0:KF * BLK], ACT.Copy).then_inc(ht_ready, 1)
                act.wait_ge(y_done, b + 1)
                if not first:
                    act.wait_ge(y_out, 16 * b)
                nc.scalar.activation(yb[0:BLK, :], ps[0:BLK, 2, :], ACT.Copy).then_inc(y_evac, 1)

            expert_block(0, True)
            with act.Fori(1, total) as b:
                expert_block(b, False)
            for t in range(NT):
                act.wait_ge(xf_done, t + 1)
                if t >= 1:
                    act.wait_ge(sqf, t)
                nc.scalar.activation(junk, x[:, t, :], ACT.Square, accum_out=ssf[:, t:t + 1]).then_inc(sqf, 1)

        @block.vector
        def _(dve):
            n_link = [0]

            def link(ins):
                n_link[0] += 1
                ins.then_inc(dch, 1)
                dve.wait_ge(dch, n_link[0])

            nc.vector.memset(zpad, 0.0)
            link(nc.vector.memset(zeros[:], 0.0))
            nc.vector.memset(zeros[:, 0:1], 0.0).then_inc(zeros_ready, 1)
            dve.wait_ge(n1_in, 16)
            for t in range(NT + 1):
                if t < NT:
                    dve.wait_ge(root1, t + 1)
                    if t >= 2:
                        dve.wait_ge(xps, t - 1)
                    nc.vector.scalar_tensor_tensor(xs[:, t % 2, :], x[:, t, :], r1[:, t:t + 1], n1,
                                                   ALU.mult, ALU.mult).then_inc(xs_ready, 1)
                if t >= 1:
                    q = t - 1
                    dve.wait_ge(hhi_done, q + 1)
                    src = ps[:, 2 + 2 * (q % 2):4 + 2 * (q % 2), :].rearrange("p a (k n) -> p (a k) n", n=P)
                    cols = slice(q * P, (q + 1) * P)
                    nc.vector.tensor_tensor(hT[:, 1, :, cols], src, fp32(hT[:, 0, :, cols]), ALU.subtract).then_inc(h_ready, 1)
            dve.wait_ge(vec_in, 16)

            def glu(c, g, half):
                kind, i = CHUNKS[c]
                if kind != "conv" or g < 2 or half == 0:
                    return
                m = 2 * i + g % 2
                dve.wait_ge(win_done, GROUP_AT[c, g] + 1)
                dve.wait_ge(sig_ready, m + 1)
                at, R, n, cols = (HALO + LS + HALO, RP, LP, slice(LS, T)) if g % 2 else (HALO, RS, LS, slice(0, LS))
                nc.vector.tensor_tensor(zpad[:, i % 2, at:at + n].rearrange("p (r c) -> p c r", c=GRID),
                                        ps[:, g % 2, 0:n].rearrange("p (c r) -> p c r", r=R),
                                        sig[:, cols].rearrange("p (c r) -> p c r", r=R), ALU.mult).then_inc(z_done, 1)
                dve.wait_ge(z_done, m + 1)

            def lo_of_run(run):
                dve.wait_ge(hi_done, run + 1)
                hi, lo = w_split[:, run % 2, 0], w_split[:, run % 2, 1]
                nc.vector.tensor_tensor(lo, w_raw[:, run % 2], fp32(hi), ALU.subtract).then_inc(split_done["dve"], 1)

            def tap(j, k):
                z = zpad[:, j % 2, k:k + CW]
                w = vec[:, V_CW + TAPS * j + k:V_CW + TAPS * j + k + 1]
                if k == 0:
                    link(nc.vector.tensor_scalar(conv[:, j % 2, :], z, w, vec[:, V_CB + j:V_CB + j + 1], ALU.mult, ALU.add))
                elif k < TAPS - 1:
                    link(nc.vector.scalar_tensor_tensor(conv[:, j % 2, :], z, w, conv[:, j % 2, :], ALU.mult, ALU.add))
                else:
                    for at, to, R in ((0, 0, RS), (LS + HALO, LS, RP)):
                        n = R * GRID
                        ins = nc.vector.scalar_tensor_tensor(
                            conv_out[:, j, to:to + n].rearrange("p (c r) -> p r c", r=R),
                            z[:, at:at + n].rearrange("p (r c) -> p r c", c=GRID), w,
                            conv[:, j % 2, at:at + n].rearrange("p (r c) -> p r c", c=GRID), ALU.mult, ALU.add)
                    ins.then_inc(conv_done, 1)
                    dve.wait_ge(conv_done, j + 1)

            def shifted(u):
                h, t = divmod(u, NT)
                dve.wait_ge(s_done, u + 1)
                if t == 0:
                    dve.wait_ge(bias_ready, h + 1)
                if u >= 2:
                    dve.wait_ge(exp_done, u - 1)
                nc.vector.tensor_tensor_reduce(out=neg_s[:, u % 2, :], in0=ps[:, 2 + u % 2, 0:256],
                                               in1=bias[:, h % 2, VARIANT_OF[t], :], scale=-1.0, scalar=3e38,
                                               op0=ALU.add, op1=ALU.min,
                                               accum_out=nmax[:, u % 2:u % 2 + 1]).then_inc(neg_done, 1)

            def head_out(h):
                dve.wait_ge(o_done, NT * (h + 1))
                link(nc.vector.reciprocal(rinv[:, h % 2, :], rsum[:, h % 2, :]))
                nc.vector.tensor_tensor(attn[:, :, h * DH:(h + 1) * DH],
                                        ps[:, 6 + h % 2, 0:NT * DH].rearrange("p (t d) -> p t d", t=NT),
                                        rinv[:, h % 2, :].unsqueeze(2).to_broadcast([P, NT, DH]),
                                        ALU.mult).then_inc(attn_done, 1)

            def moments(t):
                dve.wait_ge(ct_done, t + 1)
                link(nc.vector.bn_stats(bst[:, t, :], ps[:, 0, :]))
                nc.vector.bn_aggr(mv[:, t, :], bst[:, t, :]).then_inc(stat_done, 1)

            def normed(t):
                dve.wait_ge(rootl, t + 1)
                nc.vector.tensor_scalar(zn[:, t, :], ps[:, 0, :], mv[:, t, 0:1], rl[:, t:t + 1],
                                        ALU.subtract, ALU.mult).then_inc(zn_ready, 1)

            def with_gain(piece):
                n = PIECE[piece]
                what, u = piece
                if 2 <= n < 2 + 2 * JC:
                    dve.wait_ge(m_done, n - 1)
                elif n >= 2:
                    dve.wait_ge(mc_done, u - 1)
                if what == "cg":
                    dve.wait_ge(silu_done, JC * (u + 1))
                    g = vec[:, V_GO + JC:V_GO + KD]
                    ins = nc.vector.tensor_tensor(gained[:, n % 2, :].rearrange("p (j n) -> p j n", j=JC),
                                                  zn[:, u, :].rearrange("p (j n) -> p j n", j=JC),
                                                  g.unsqueeze(2).to_broadcast([P, JC, P]), ALU.mult)
                else:
                    dve.wait_ge(at_done, u + 1)
                    ins = nc.vector.tensor_scalar(gained[:, n % 2, 0:3 * P], ps[:, u % 2, 0:3 * P],
                                                  vec[:, V_GO + u // 2:V_GO + u // 2 + 1], None, ALU.mult)
                ins.then_inc(gained_done, 1)

            def lo_of_conv(t):
                n = PIECE["cg", t]
                dve.wait_ge(mhi_done, n + 1)
                cols = slice(t * P, (t + 1) * P)
                nc.vector.tensor_tensor(mT[:, 1, JC:, cols], gained[:, n % 2, :].rearrange("p (j n) -> p j n", j=JC),
                                        fp32(mT[:, 0, JC:, cols]), ALU.subtract).then_inc(mc_done, 1)

            for what, *a in ORDER:
                if what == "win":
                    glu(*a)
                elif what == "split" and a[0] in BY_DVE:
                    lo_of_run(*a)
                elif what == "tap":
                    tap(*a)
                elif what == "att":
                    k, = a
                    if k < H * NT:
                        shifted(k)
                    if k >= 2 and (k - 2) % NT == NT - 1:
                        head_out((k - 2) // NT)
                elif what == "ln":
                    moments(*a)
                elif what == "zn":
                    normed(*a)
                elif what in ("cg", "at"):
                    with_gain((what, *a))
                elif what == "lo":
                    lo_of_conv(*a)

            dve.wait_ge(ssc_done, NT)
            nc.vector.tensor_copy(ssc[:], ps[:, 0, 0:NT]).then_inc(ssc_ready, 1)
            dve.wait_ge(roota, 1)
            dve.wait_ge(rootc, 1)
            for n in range(OUT_CHUNKS):
                for t in range(NT):
                    g = n * NT + t
                    dve.wait_ge(wout_done, g + 1)
                    if n == 0:
                        dve.wait_ge(x_in[t], 32)
                    xn = x[:, t, 2 * P * n:2 * P * (n + 1)]
                    link(nc.vector.scalar_tensor_tensor(xn, ps[:, 2 + g % 2, 0:2 * P], ra[:, t:t + 1], xn, ALU.mult, ALU.add))
                    nc.vector.scalar_tensor_tensor(xn, ps[:, 2 + g % 2, 2 * P:], rc[:, t:t + 1], xn,
                                                   ALU.mult, ALU.add).then_inc(x2_done, 1)
            dve.wait_ge(n2_in, 16)
            for t in range(NT):
                dve.wait_ge(root2, t + 1)
                nc.vector.scalar_tensor_tensor(h2[:, t, :], x[:, t, :], r2[:, t:t + 1], n2[:],
                                               ALU.mult, ALU.mult).then_inc(h2_ready, 1)
            dve.wait_ge(lg_done, NT)
            dve.wait_ge(small_in, 32)
            V = nc.vector

            def over(a, n):
                return a.unsqueeze(2).to_broadcast([P, NT, n])

            def same(a, shape):
                return a.unsqueeze(1).to_broadcast([P, NT, shape])

            def first_max(onehot, values, top, order, tmp, n):
                link(V.tensor_reduce(top, values, AX.X, ALU.max))
                link(V.tensor_tensor(tmp, values, over(top, n), ALU.is_equal))
                link(V.tensor_tensor(tmp, tmp, same(order, n), ALU.mult))
                link(V.tensor_reduce(t1[:], tmp, AX.X, ALU.max))
                link(V.tensor_tensor(onehot, tmp, over(t1[:], n), ALU.is_equal))

            link(V.tensor_tensor(lg[:], ps[:, 6, 0:NT * NR].rearrange("p (t n) -> p t n", t=NT), same(br[:], NR), ALU.add))
            first_max(ohg[:], lg[:, :, 0:G], g1[:], w4[:], t4[:], G)
            V.tensor_tensor(gd[:], lg[:, :, 0:G], over(g1[:], G), ALU.subtract).then_inc(gd_ready, 1)
            for g in range(G):
                lge = lg[:, :, G + g * EG:G + (g + 1) * EG]
                link(V.tensor_tensor(el[:, :, g, :], lge, over(ohg[:, :, g], EG), ALU.mult))
            link(V.tensor_tensor(es[:], el[:, :, 0, :], el[:, :, 1, :], ALU.add))
            link(V.tensor_tensor(es[:], es[:], el[:, :, 2, :], ALU.add))
            link(V.tensor_tensor(es[:], es[:], el[:, :, 3, :], ALU.add))
            first_max(oh[:, 0, :, :], es[:], m1[:], w8[:], t8[:], EG)
            link(V.scalar_tensor_tensor(es2[:], oh[:, 0, :, :], -3e38, es[:], ALU.mult, ALU.add))
            first_max(oh[:, 1, :, :], es2[:], m2[:], w8[:], t8[:], EG)
            V.tensor_tensor(dd[:], m2[:], m1[:], ALU.subtract).then_inc(dd_ready, 1)
            for j in range(2):
                for g in range(G):
                    link(V.tensor_tensor(sel[:, j, :, g * EG:(g + 1) * EG], oh[:, j, :, :], over(ohg[:, :, g], EG), ALU.mult))
            link(V.memset(both[:, NT, :], 0.0))
            link(V.tensor_tensor(both[:, 0:NT, :], sel[:, 0, :, :], sel[:, 1, :, :], ALU.add))
            link(V.memset(before[:, 0, :], 0.0))
            for t in range(NT):
                ins = V.tensor_tensor(before[:, t + 1, :], before[:, t, :], both[:, t, :], ALU.add)
                if t < NT - 1:
                    link(ins)
            ins.then_inc(both_ready, 1)
            dve.wait_ge(ge_ready, 1)
            link(V.tensor_reduce(gpi[:], ge[:], AX.X, ALU.add))
            link(V.reciprocal(gp[:], gpi[:]))
            dve.wait_ge(ex_ready, 1)
            link(V.tensor_scalar(gate2[:], ex[:], 1.0, None, ALU.add))
            link(V.reciprocal(gate1[:], gate2[:]))
            link(V.tensor_tensor(gate1[:], gate1[:], gp[:], ALU.mult))
            link(V.tensor_tensor(gate2[:], gate1[:], ex[:], ALU.mult))
            dve.wait_ge(rank_done, 1)
            link(V.tensor_copy(cnt[:], ps[:, 0, NT * E:(NT + 1) * E]))
            link(V.tensor_tensor(cmpb, cnt[:].unsqueeze(2).to_broadcast([P, E, MAXN - 1]),
                                 thr[:].unsqueeze(1).to_broadcast([P, E, MAXN - 1]), ALU.is_gt))
            link(V.tensor_reduce(nblk[:], cmpb, AX.X, ALU.add))
            link(V.tensor_scalar(nblk[:], nblk[:], 1.0, None, ALU.add))
            link(V.tensor_tensor_scan(endb[:], onesr[:], nblk[:], 0.0, ALU.mult, ALU.add))
            link(V.tensor_tensor(st64[:], endb[:], nblk[:], ALU.subtract))
            link(V.tensor_copy(table[0:1, 0:E], nblk[0:1, :]))
            link(V.tensor_copy(table[0:1, E:2 * E], st64[0:1, :]))
            link(V.tensor_scalar(st64[:], st64[:], float(BLK), None, ALU.mult))
            link(V.tensor_tensor(pos, ps[:, 0, 0:NT * E].rearrange("p (t e) -> p t e", t=NT), same(st64[:], E), ALU.add))
            for j in range(2):
                link(V.tensor_tensor(posd, sel[:, j, :, :], pos, ALU.mult))
                link(V.tensor_reduce(destf[:, j, :], posd, AX.X, ALU.add))
            V.tensor_copy(dest[:], destf[:]).then_inc(dest_ready, 1)
            V.memset(t1[:], 0.0).then_inc(y_evac, 1)
            V.tensor_copy(table[0:1, 2 * E:3 * E], endb[0:1, :]).then_inc(table_ready, 1)

            dve.wait_ge(table_ready, 1)
            total = dve.value_load(table[0:1, 3 * E - 1:3 * E], min_val=E, max_val=MAXB)

            def rows_in(b):
                dve.wait_ge(xt_ps, b + 1)
                nc.vector.tensor_copy(xT.rearrange("p k n -> p (k n)"), ps[:, 4, :]).then_inc(xt_ready, 1)

            def expert_block(b, first):
                dve.wait_ge(sg_ready, b + 1)
                nc.vector.tensor_tensor(hb, ps[BLK:2 * BLK, 1, :], sG, ALU.mult).then_inc(hb_ready, 1)
                rows_in(b + 1)
                dve.wait_ge(y_done, b + 1)
                if not first:
                    dve.wait_ge(y_out, 16 * b)
                nc.vector.tensor_copy(yb[BLK:2 * BLK, :], ps[BLK:2 * BLK, 3, :]).then_inc(y_evac, 1)

            rows_in(0)
            expert_block(0, True)
            with dve.Fori(1, total) as b:
                expert_block(b, False)

            dve.wait_ge(fin_in, 16)
            for t in range(NT + 1):
                if t < NT:
                    dve.wait_ge(gath_in[t], 32)
                    link(nc.vector.scalar_tensor_tensor(x[:, t, :], gath[:, t, 0, :], gate1[:, t:t + 1], x[:, t, :],
                                                        ALU.mult, ALU.add))
                    nc.vector.scalar_tensor_tensor(x[:, t, :], gath[:, t, 1, :], gate2[:, t:t + 1], x[:, t, :],
                                                   ALU.mult, ALU.add).then_inc(xf_done, 1)
                if t >= 1:
                    dve.wait_ge(rootf, t)
                    nc.vector.scalar_tensor_tensor(x[:, t - 1, :], x[:, t - 1, :], rf[:, t - 1:t], fin_g,
                                                   ALU.mult, ALU.mult).then_inc(fin_done, 1)


def kernel(x_prompt, x_sample, norm1_g, w_in, rpb, attn_out_g, conv_w, conv_b, conv_ln_g, conv_ln_b, conv_out_g,
           w_out, norm2_g, w_group, b_group, w_expert, b_expert, w_e_gate, w_e_up, w_e_down, final_g):
    import concourse.bacc as bacc
    from concourse.bass_utils import run_bass_kernel_spmd

    def by_partition(a):
        return np.ascontiguousarray(np.asarray(a).reshape(-1, P).T)

    taps = np.asarray(conv_w)[0].reshape(TAPS, JC, P).transpose(2, 1, 0).reshape(P, JC * TAPS)
    vectors = np.concatenate([taps, by_partition(conv_b), by_partition(conv_ln_g),
                              by_partition(conv_ln_b), by_partition(attn_out_g), by_partition(conv_out_g)], axis=1)
    router = np.concatenate([np.asarray(w_group)[0], np.asarray(w_expert)[0].transpose(1, 0, 2).reshape(D, E)], axis=1)
    router = router.reshape(KD, P, NR).transpose(1, 0, 2).reshape(P, KD * NR)
    router_b = np.concatenate([np.asarray(b_group)[0], np.asarray(b_expert)[0].reshape(E)])
    side = (RPBW - np.shape(rpb)[3]) // 2
    arrays = {
        "x_prompt": x_prompt, "x_sample": x_sample, "norm1": norm1_g, "w_in": w_in,
        "rpb": np.pad(np.asarray(rpb)[0], ((0, 0), (0, 0), (side, side))),
        "vectors": vectors, "w_out": w_out, "norm2": norm2_g, "router_w": router, "router_b": router_b,
        "w_gate": w_e_gate, "w_up": w_e_up, "w_down": w_e_down, "final_g": final_g,
    }
    nc = bacc.Bacc("TRN2", target_bir_lowering=False, num_devices=1)
    ins, args = {}, []
    for name, a in arrays.items():
        a = np.ascontiguousarray(a)
        ins["in_" + name] = a
        args.append(nc.dram_tensor("in_" + name, a.shape, mybir.dt.from_np(a.dtype), kind="ExternalInput").ap())
    for name, like in (("y_prompt", x_prompt), ("y_sample", x_sample)):
        args.append(nc.dram_tensor("out_" + name, np.shape(like), F32, kind="ExternalOutput").ap())
    encoder(nc, *args)
    r = run_bass_kernel_spmd(nc, [ins], core_ids=[0]).results[0]
    return r["out_y_prompt"], r["out_y_sample"]
```
